# Optimizing a Trainium2 kernel written in Bass

```python
import math
import jax, jax.numpy as jnp
from jax import lax
import numpy as np

D_MODEL = 1024
BATCH = 1
SEQ = 256
DEPTH = 2

CHUNK = 64
N_A_LAYERS = max(1, DEPTH // 2)
N_B_LAYERS = DEPTH - N_A_LAYERS
N_HEADS = 16
HEAD_DIM = D_MODEL // N_HEADS
Q_BLOCK = 128
CONV_K = 31
N_EXPERTS = 16
N_GROUPS = 4
EXPERTS_PER_GROUP = N_EXPERTS // N_GROUPS
TOP_K = 2
D_EXPERT = D_MODEL
MOE_BLOCK = 256
ALPHA = (2.0 * DEPTH) ** 0.25
BETA = (8.0 * DEPTH) ** -0.25
LN_EPS = 1e-5

kernel_name = "yoco_conformer_fox_grouped_moe_deepnorm"

def layer_norm(x, g, b):
    xf = x.astype(jnp.float32)
    mu = xf.mean(-1, keepdims=True)
    var = jnp.square(xf - mu).mean(-1, keepdims=True)
    return ((xf - mu) * lax.rsqrt(var + LN_EPS)).astype(x.dtype) * g + b

def conformer_conv(h, w_pw1, b_pw1, w_dw, b_dw, ln_g, ln_b, w_pw2, b_pw2):
    D = h.shape[-1]
    u = h @ w_pw1 + b_pw1
    u = u[..., :D] * jax.nn.sigmoid(u[..., D:])
    y = lax.conv_general_dilated(
        u, w_dw, window_strides=(1,), padding=[(CONV_K - 1, 0)],
        dimension_numbers=('NWC', 'WIO', 'NWC'), feature_group_count=D) + b_dw
    y = jax.nn.silu(layer_norm(y, ln_g, ln_b))
    return y @ w_pw2 + b_pw2

def shared_kv(x, c_act, w_ada_kv, b_ada_kv, w_kvf, b_f):
    B, S, D = x.shape
    shift, scale = jnp.split((c_act @ w_ada_kv + b_ada_kv)[:, None, :], 2, axis=-1)
    hk = x * (1 + scale) + shift
    kvf = hk @ w_kvf
    k = kvf[..., :D].reshape(B, S, N_HEADS, HEAD_DIM)
    v = kvf[..., D:2 * D].reshape(B, S, N_HEADS, HEAD_DIM)
    log_f = jax.nn.log_sigmoid((kvf[..., 2 * D:] + b_f).astype(jnp.float32))
    fcum = jnp.cumsum(log_f, axis=1).transpose(0, 2, 1)
    return k, v, fcum

def fox_attention(q, k, v, fcum):
    S = q.shape[1]
    scale = HEAD_DIM ** -0.5
    outs = []
    for i in range(S // Q_BLOCK):
        q0, q1 = i * Q_BLOCK, (i + 1) * Q_BLOCK
        s = jnp.einsum('bqhd,bkhd->bhqk', q[:, q0:q1], k[:, :q1]).astype(jnp.float32) * scale
        s = s + fcum[:, :, q0:q1, None] - fcum[:, :, None, :q1]
        causal = (q0 + jnp.arange(Q_BLOCK))[:, None] >= jnp.arange(q1)[None, :]
        s = jnp.where(causal, s, -jnp.inf)
        p = jax.nn.softmax(s, axis=-1).astype(v.dtype)
        outs.append(jnp.einsum('bhqk,bkhd->bqhd', p, v[:, :q1]))
    return jnp.concatenate(outs, axis=1)

def grouped_moe(h, router_w, router_b, w_gate, w_up, w_down):
    B, S, D = h.shape
    N = B * S
    t = h.reshape(N, D)
    logits = (t @ router_w).astype(jnp.float32) + router_b.astype(jnp.float32)
    probs = jax.nn.softmax(logits, axis=-1).reshape(N, N_GROUPS, EXPERTS_PER_GROUP)
    group_score = lax.top_k(probs, TOP_K)[0].sum(-1)
    g_sel = jnp.argmax(group_score, axis=-1)
    in_group = jnp.take_along_axis(probs, g_sel[:, None, None], axis=1)[:, 0]
    w_top, i_top = lax.top_k(in_group, TOP_K)
    w_top = w_top / w_top.sum(-1, keepdims=True)
    expert_idx = (g_sel[:, None] * EXPERTS_PER_GROUP + i_top).reshape(-1)
    tok_idx = jnp.repeat(jnp.arange(N, dtype=jnp.int32), TOP_K)
    gate_w = w_top.reshape(-1)
    A = N * TOP_K
    order = jnp.argsort(expert_idx)
    e_sorted = expert_idx[order]
    counts = jnp.bincount(expert_idx, length=N_EXPERTS)
    padded = (counts + MOE_BLOCK - 1) // MOE_BLOCK * MOE_BLOCK
    pad_end = jnp.cumsum(padded)
    pad_start = pad_end - padded
    start = jnp.cumsum(counts) - counts
    dest = pad_start[e_sorted] + jnp.arange(A) - start[e_sorted]
    n_blocks = -(-A // MOE_BLOCK) + N_EXPERTS
    P = n_blocks * MOE_BLOCK
    slot_tok = jnp.full((P,), N, jnp.int32).at[dest].set(tok_idx[order])
    slot_w = jnp.zeros((P,), jnp.float32).at[dest].set(gate_w[order])
    block_expert = jnp.minimum(
        jnp.searchsorted(pad_end, jnp.arange(n_blocks) * MOE_BLOCK, side='right'), N_EXPERTS - 1)
    t_pad = jnp.concatenate([t, jnp.zeros((1, D), t.dtype)], axis=0)
    xs = t_pad[slot_tok].reshape(n_blocks, MOE_BLOCK, D)

    def expert_block(args):
        xb, e = args
        return (jax.nn.silu(xb @ w_gate[e]) * (xb @ w_up[e])) @ w_down[e]

    ys = lax.map(expert_block, (xs, block_expert)).reshape(P, D)
    ys = ys * slot_w[:, None].astype(ys.dtype)
    out = jnp.zeros((N + 1, D), ys.dtype).at[slot_tok].add(ys)[:N]
    return out.reshape(B, S, D)

def setup_inputs(seed: int = 0) -> dict:
    key = jax.random.key(seed)
    ks = jax.random.split(key, 32)
    D, H, F, E = D_MODEL, N_HEADS, D_EXPERT, N_EXPERTS
    f32 = jnp.float32

    def nrm(i, shape, scale):
        return jax.random.normal(ks[i], shape, f32) * scale

    w_kvf = jnp.concatenate([
        nrm(20, (D, D), D ** -0.5),
        nrm(21, (D, D), BETA * D ** -0.5),
        nrm(22, (D, H), 0.1 * D ** -0.5)], axis=1)
    return {
        "x": nrm(0, (BATCH, SEQ, D), 1.0),
        "c": nrm(1, (BATCH, D), 1.0),
        "w_ada": nrm(2, (DEPTH, D, 6 * D), 0.1 * D ** -0.5),
        "b_ada": nrm(3, (DEPTH, 6 * D), 0.01),
        "ln_mix_g": 1.0 + nrm(4, (DEPTH, D), 0.02),
        "ln_mix_b": nrm(5, (DEPTH, D), 0.02),
        "ln_ffn_g": 1.0 + nrm(6, (DEPTH, D), 0.02),
        "ln_ffn_b": nrm(7, (DEPTH, D), 0.02),
        "w_pw1": nrm(8, (N_A_LAYERS, D, 2 * D), D ** -0.5),
        "b_pw1": nrm(9, (N_A_LAYERS, 2 * D), 0.01),
        "w_dw": nrm(10, (N_A_LAYERS, CONV_K, 1, D), CONV_K ** -0.5),
        "b_dw": nrm(11, (N_A_LAYERS, D), 0.01),
        "conv_ln_g": 1.0 + nrm(12, (N_A_LAYERS, D), 0.02),
        "conv_ln_b": nrm(13, (N_A_LAYERS, D), 0.02),
        "w_pw2": nrm(14, (N_A_LAYERS, D, D), BETA * D ** -0.5),
        "b_pw2": nrm(15, (N_A_LAYERS, D), 0.01),
        "w_ada_kv": nrm(16, (D, 2 * D), 0.1 * D ** -0.5),
        "b_ada_kv": nrm(17, (2 * D,), 0.01),
        "w_kvf": w_kvf,
        "b_f": 1.0 + 4.0 * jax.random.uniform(ks[23], (H,), f32),
        "w_q": nrm(24, (N_B_LAYERS, D, D), D ** -0.5),
        "w_o": nrm(25, (N_B_LAYERS, D, D), BETA * D ** -0.5),
        "router_w": nrm(26, (D, E), D ** -0.5),
        "router_b": nrm(27, (E,), 0.01),
        "w_gate": nrm(28, (DEPTH, E, D, F), D ** -0.5),
        "w_up": nrm(29, (DEPTH, E, D, F), D ** -0.5),
        "w_down": nrm(30, (DEPTH, E, F, D), BETA * F ** -0.5),
    }

def reference(x, c, w_ada, b_ada, ln_mix_g, ln_mix_b, ln_ffn_g, ln_ffn_b,
              w_pw1, b_pw1, w_dw, b_dw, conv_ln_g, conv_ln_b, w_pw2, b_pw2,
              w_ada_kv, b_ada_kv, w_kvf, b_f, w_q, w_o,
              router_w, router_b, w_gate, w_up, w_down):
    B, S, D = x.shape
    c_act = jax.nn.silu(c)
    k = v = fcum = None
    for l in range(DEPTH):
        mod = (c_act @ w_ada[l] + b_ada[l])[:, None, :]
        sh1, sc1, g1, sh2, sc2, g2 = jnp.split(mod, 6, axis=-1)
        h = x * (1 + sc1) + sh1
        if l < N_A_LAYERS:
            y = conformer_conv(h, w_pw1[l], b_pw1[l], w_dw[l], b_dw[l],
                               conv_ln_g[l], conv_ln_b[l], w_pw2[l], b_pw2[l])
        else:
            if l == N_A_LAYERS:
                k, v, fcum = shared_kv(x, c_act, w_ada_kv, b_ada_kv, w_kvf, b_f)
            j = l - N_A_LAYERS
            q = (h @ w_q[j]).reshape(B, S, N_HEADS, HEAD_DIM)
            y = fox_attention(q, k, v, fcum).reshape(B, S, D) @ w_o[j]
        x = layer_norm(ALPHA * x + (1 + g1) * y, ln_mix_g[l], ln_mix_b[l])
        h = x * (1 + sc2) + sh2
        y = grouped_moe(h, router_w, router_b, w_gate[l], w_up[l], w_down[l])
        x = layer_norm(ALPHA * x + (1 + g2) * y, ln_ffn_g[l], ln_ffn_b[l])
    return x


_drawn_inputs = setup_inputs


def setup_inputs(seed=0):
    import zlib

    import numpy as np

    out = dict(_drawn_inputs(seed))
    spreads = {}
    factors = {'b_pw1': 3.617, 'conv_ln_g': 3.615, 'b_ada_kv': 4.046}
    for name, (base, spread) in spreads.items():
        noise = np.random.default_rng([zlib.crc32(name.encode()), seed]).standard_normal(out[name].shape)
        drawn = base * np.exp(spread * noise) if base else spread * noise
        out[name] = __import__('jax').numpy.asarray(drawn.astype(out[name].dtype))
    for name, factor in factors.items():
        out[name] = (out[name] * factor).astype(out[name].dtype)
    return out
```

```python
import math
from contextlib import ExitStack

import concourse.bass as bass
from concourse import mybir

F32 = mybir.dt.float32
I32 = mybir.dt.int32
ALU = mybir.AluOpType
ACT = mybir.ActivationFunctionType
AX = mybir.AxisListType

P = 128
BANK = 512
SLOTS = 64
RING = 8
MASKED = -1e30
LN_EPS = 1e-5


def trunk_kernel(nc, x, c, w_ada, b_ada, ln_mix_g, ln_mix_b, ln_ffn_g, ln_ffn_b,
                 w_pw1, b_pw1, w_dw, b_dw, conv_ln_g, conv_ln_b, w_pw2, b_pw2,
                 w_ada_kv, b_ada_kv, w_kvf, b_f, w_q, w_o,
                 router_w, router_b, w_gate, w_up, w_down, out):
    DEPTH, E, D, F = w_gate.shape
    SEQ = x.shape[1]
    TAPS = w_dw.shape[1]
    HEADS = b_f.shape[0]
    HD = D // HEADS
    GROUPS, PER = 4, 4
    TT = SEQ // P
    KD = D // P
    KH = KD // 2
    HALF = D // 2
    PAD = TAPS - 1
    ALPHA = (2.0 * DEPTH) ** 0.25
    assert (D, F, TT, HD, E, DEPTH) == (1024, 1024, 2, 64, GROUPS * PER, 2)
    assert HALF == BANK and SLOTS * 2 == P

    ROW_BA, ROW_BB, ROW_BDW, ROW_LNG, ROW_LNB, ROW_C = range(TAPS, TAPS + 6)
    NROWS = TAPS + 6

    ADA_G = 4
    L_ADA0_G0 = 0
    L_PW1 = L_ADA0_G0 + ADA_G
    L_ADA0_G1 = L_PW1 + 4
    L_ADA0_G2 = L_ADA0_G1 + ADA_G
    L_PW2 = L_ADA0_G2 + ADA_G
    L_MOE0 = L_PW2 + 2
    L_ADAKV = L_MOE0 + 6 * E
    L_ADA1_G0 = L_ADAKV + ADA_G
    L_WK = L_ADA1_G0 + ADA_G
    L_WV = L_WK + 2
    L_WQ = L_WV + 2
    L_ADA1_G1 = L_WQ + 2
    L_ADA1_G2 = L_ADA1_G1 + ADA_G
    L_WO = L_ADA1_G2 + ADA_G
    L_MOE1 = L_WO + 2
    UNROLL = 4
    TURN = 6 * UNROLL
    assert TURN % RING == 0 and E % UNROLL == 0

    def halves(w, rows_first=0):
        return w.rearrange("(h k p) f -> h p k f", h=2, p=P)

    wide_ada = [[w_ada[l, :, g * 2048:(g + 1) * 2048].rearrange("(j k p) f -> j p k f", k=2, p=P)
                 for g in range(3)] for l in range(DEPTH)]
    wide_kv = w_ada_kv.rearrange("(j k p) f -> j p k f", k=2, p=P)
    wide_pw1 = w_pw1[0].rearrange("(j k p) f -> j p k f", k=2, p=P)
    pw2_h = halves(w_pw2[0])
    wk_h = halves(w_kvf[:, 0:D])
    wv_h = halves(w_kvf[:, D:2 * D])
    wq_h = halves(w_q[0])
    wo_h = halves(w_o[0])
    gate_h = w_gate.rearrange("l e (h k p) f -> (l e) h p k f", h=2, p=P)
    up_h = w_up.rearrange("l e (h k p) f -> (l e) h p k f", h=2, p=P)
    down_h = w_down.rearrange("l e (h k p) f -> (l e) h p k f", h=2, p=P)

    ctx = ExitStack()
    with ctx:
        def sb(name, shape, dt=F32):
            return ctx.enter_context(nc.sbuf_tensor(name, shape, dt))

        def sem(name):
            return ctx.enter_context(nc.semaphore(name))

        ring = sb("ring", [P, RING, KH * D])
        xs = sb("xs", [P, TT, D])
        hs = sb("hs", [P, TT, D])
        hT = sb("hT", [P, KD, SEQ])
        work = sb("work", [P, 7168])
        modv = [sb(f"modv{l}", [P, 3, BANK]) for l in range(DEPTH)]
        modkv = sb("modkv", [P, 1, BANK])
        lnrows = sb("lnrows", [P, D])
        colv = sb("colv", [P, KD, NROWS])
        cact = sb("cact", [P, KD])
        crep = sb("crep", [P, KD, 32])
        rw = sb("rw", [P, KD, E])
        rbias = sb("rbias", [P, E])
        wf = sb("wf", [P, KD, HEADS])
        bf = sb("bf", [HEADS, 1])
        ident = sb("ident", [P, P])
        before = sb("before", [P, P])
        upto = sb("upto", [P, P])
        ones = sb("ones", [P, P])
        ones_d = sb("ones_d", [P, P])
        slot1 = sb("slot1", [P, SEQ])
        slot1i = sb("slot1i", [P, SEQ], I32)
        cmask = sb("cmask", [P, P])
        plus1 = sb("plus1", [P, 3])
        later = sb("later", [P, 2 * GROUPS, PER])
        eps = sb("eps", [P, 1])
        stats = sb("stats", [P, TT, 2, 6])
        mv = sb("mv", [P, TT, 2])
        rstd = sb("rstd", [P, TT])
        r_ex = sb("r_ex", [P, TT, E])
        r_p = sb("r_p", [P, TT, E])
        r_c = sb("r_c", [P, 2 * GROUPS, PER])
        r_rk = sb("r_rk", [P, 2 * GROUPS, PER])
        r_sel = sb("r_sel", [P, TT, E])
        r_gs = sb("r_gs", [P, TT, GROUPS])
        r_gc = sb("r_gc", [P, TT, GROUPS])
        r_gr = sb("r_gr", [P, TT, GROUPS])
        r_w = sb("r_w", [P, TT, E])
        r_pos = sb("r_pos", [P, TT, E])
        r_s = sb("r_s", [P, TT])
        r_n = sb("r_n", [1, E])
        blocks_i = sb("blocks_i", [1, E], I32)

        at = [0]

        def part(n, **kw):
            a = work[:, at[0]:at[0] + n]
            at[0] += n
            return a.rearrange(kw["to"], **{k: v for k, v in kw.items() if k != "to"}) if kw else a

        Xg = part(BANK)
        XT = part(BANK, to="p (c s) -> p c s", c=KH)
        sil = part(BANK)
        hh = part(BANK)
        hhT = part(BANK, to="p (c s) -> p c s", c=KH)
        yb = part(BANK)
        G = part(TT * SLOTS, to="p (t s) -> p t s", t=TT)
        GW = part(TT * P, to="p (t q s) -> p t q s", t=TT, q=2)
        GWT = part(SEQ)
        at[0] = 0
        U = part(KD * (SEQ + PAD), to="p (k t) -> p k t", k=KD)
        CV = part(KD * SEQ, to="p (k t) -> p k t", k=KD)
        colrows = part(D)
        brow = part(D)
        SG = part(2 * SEQ, to="p (b t) -> p b t", b=2)
        crstd = part(SEQ)
        at[0] = 0
        KT = part(KD * SEQ, to="p (k t) -> p k t", k=KD)
        QT = part(KD * SEQ, to="p (k t) -> p k t", k=KD)
        V = part(TT * D, to="p (t d) -> p t d", t=TT)
        fz = part(SEQ)
        fe = part(SEQ)
        fl = part(SEQ)
        nfc = part(SEQ)
        hflat = hs[:, :, :].rearrange("p t d -> p (t d)")
        PR = hflat[:, 0:768].rearrange("p (b n) -> p b n", b=2)
        PRT = hflat[:, 768:1536].rearrange("p (b n) -> p b n", b=2)
        ltok = hflat[:, 1536:1568].rearrange("p (t h) -> p t h", t=TT)
        fq = hflat[:, 1568:1600].rearrange("p (t h) -> p t h", t=TT)
        rmax = hflat[:, 1600:1632].rearrange("p (t h) -> p t h", t=TT)
        nmax = hflat[:, 1632:1664].rearrange("p (t h) -> p t h", t=TT)
        rsum = hflat[:, 1664:1696].rearrange("p (t h) -> p t h", t=TT)
        rinv = hflat[:, 1696:1728].rearrange("p (t h) -> p t h", t=TT)

        PS = ctx.enter_context(nc.psum_tensor("PS", [P, 8, BANK], F32))
        B_GATE, B_UP, B_Y, B_M = 4, 5, 6, 7

        landed = [sem(f"landed{i}") for i in range(RING)]
        half_free = sem("half_free")
        consts = sem("consts")
        small_in = sem("small_in")
        x_in = sem("x_in")
        rows_in = [sem(f"rows_in{l}") for l in range(DEPTH)]
        x_done = sem("x_done")
        out_done = sem("out_done")
        dchain = sem("dchain")
        cols_turned = sem("cols_turned")
        cols_copied = sem("cols_copied")
        c_acted = sem("c_acted")
        c_spread = sem("c_spread")
        ada_done = sem("ada_done")
        ada_added = sem("ada_added")
        spread = sem("spread")
        spread_used = sem("spread_used")
        h_ready = sem("h_ready")
        h_turned = sem("h_turned")
        hT_copied = sem("hT_copied")
        u_mm = sem("u_mm")
        sig_ready = sem("sig_ready")
        u_ready = sem("u_ready")
        conv_ready = sem("conv_ready")
        mean_done = sem("mean_done")
        cen_ready = sem("cen_ready")
        sq_ready = sem("sq_ready")
        var_done = sem("var_done")
        csd_ready = sem("csd_ready")
        cnorm_ready = sem("cnorm_ready")
        z_ready = sem("z_ready")
        y_ready = sem("y_ready")
        y_read = sem("y_read")
        ln_var = sem("ln_var")
        ln_sd = sem("ln_sd")
        logits_done = sem("logits_done")
        lmax_ready = sem("lmax_ready")
        lexp_ready = sem("lexp_ready")
        sel_ready = sem("sel_ready")
        pos_done = sem("pos_done")
        routed = sem("routed")
        G_built = sem("G_built")
        X_summed = sem("X_summed")
        X_copied = sem("X_copied")
        X_turned = sem("X_turned")
        XT_copied = sem("XT_copied")
        gate_done = sem("gate_done")
        sil_ready = sem("sil_ready")
        up_done = sem("up_done")
        hh_ready = sem("hh_ready")
        hh_turned = sem("hh_turned")
        hhT_copied = sem("hhT_copied")
        GW_turned = sem("GW_turned")
        GWT_copied = sem("GWT_copied")
        down_done = sem("down_done")
        yb_copied = sem("yb_copied")
        k_done = sem("k_done")
        k_copied = sem("k_copied")
        v_done = sem("v_done")
        v_copied = sem("v_copied")
        f_done = sem("f_done")
        fz_ready = sem("fz_ready")
        fe_ready = sem("fe_ready")
        fln_ready = sem("fln_ready")
        logf_ready = sem("logf_ready")
        logf_turned = sem("logf_turned")
        ltok_copied = sem("ltok_copied")
        fcum_done = sem("fcum_done")
        fcum_copied = sem("fcum_copied")
        q_done = sem("q_done")
        q_copied = sem("q_copied")
        s_done = sem("s_done")
        nmax_ready = sem("nmax_ready")
        exp_done = sem("exp_done")
        p_ready = sem("p_ready")
        p_turned = sem("p_turned")
        pT_copied = sem("pT_copied")
        o_done = sem("o_done")
        o_copied = sem("o_copied")

        CONSTS = 17
        SMALL = 16 * 23
        ROWS = 16 * 4
        SPREADS0 = 10

        block = ctx.enter_context(nc.Block())

        @block.sync
        def _(sp):
            def load(index, source, turn=0):
                if isinstance(turn, int):
                    if index + 1 > RING:
                        sp.wait_ge(half_free, index + 1 - RING)
                else:
                    sp.wait_ge(half_free, turn + (index + 1 - RING))
                n = source.shape[-2]
                sp.dma_start(ring[:, index % RING, :].rearrange("p (k f) -> p k f", k=n),
                             source).then_inc(landed[index % RING], 16)

            def load_wide(index, w):
                for j in range(ADA_G):
                    load(index + j, w[j])

            def load_pair(index, w):
                for h in range(2):
                    load(index + h, w[h])

            def load_experts(index, l):
                with sp.Fori(0, E // UNROLL) as turn:
                    for i in range(UNROLL):
                        e = turn * UNROLL + (l * E + i)
                        for m, w in enumerate((gate_h, up_h, down_h)):
                            for h in range(2):
                                load(index + 6 * i + 2 * m + h,
                                     w[bass.ds(e, 1), h].rearrange("o p k f -> (o p) k f"), turn * TURN)

            load_wide(L_ADA0_G0, wide_ada[0][0])
            load_wide(L_PW1, wide_pw1)
            load_wide(L_ADA0_G1, wide_ada[0][1])
            load_wide(L_ADA0_G2, wide_ada[0][2])
            load_pair(L_PW2, pw2_h)
            load_experts(L_MOE0, 0)
            load_wide(L_ADAKV, wide_kv)
            load_wide(L_ADA1_G0, wide_ada[1][0])
            load_pair(L_WK, wk_h)
            load_pair(L_WV, wv_h)
            load_pair(L_WQ, wq_h)
            load_wide(L_ADA1_G1, wide_ada[1][1])
            load_wide(L_ADA1_G2, wide_ada[1][2])
            load_pair(L_WO, wo_h)
            load_experts(L_MOE1, 1)

        @block.gpsimd
        def _(pool):
            pool.memset(ident[:, :], 0.0).then_inc(consts, 1)
            pool.memset(before[:, :], 1.0).then_inc(consts, 1)
            pool.memset(upto[:, :], 1.0).then_inc(consts, 1)
            pool.memset(cmask[:, :], 0.0).then_inc(consts, 1)
            pool.memset(ones[:, :], 1.0).then_inc(consts, 1)
            pool.memset(ones_d[:, :], 1.0 / D).then_inc(consts, 1)
            pool.memset(plus1[:, :], 1.0).then_inc(consts, 1)
            pool.memset(eps[:, :], LN_EPS).then_inc(consts, 1)
            pool.iota(slot1i[:, :], [[1, SEQ]], base=1, channel_multiplier=0).then_inc(consts, 1)
            for v in range(PER):
                last = pool.memset(later[:, :, v:v + 1], float(PER - 1 - v))
            last.then_inc(consts, 1)
            pool.wait_ge(consts, 10)
            pool.affine_select(out=ident[:, :], in_=ident[:, :], compare_op=ALU.not_equal, fill=1.0, base=0,
                               pattern=[[1, P]], channel_multiplier=-1).then_inc(consts, 1)
            pool.affine_select(out=before[:, :], in_=before[:, :], compare_op=ALU.is_gt, fill=0.0, base=0,
                               pattern=[[1, P]], channel_multiplier=-1).then_inc(consts, 1)
            pool.affine_select(out=upto[:, :], in_=upto[:, :], compare_op=ALU.is_ge, fill=0.0, base=0,
                               pattern=[[1, P]], channel_multiplier=-1).then_inc(consts, 1)
            pool.affine_select(out=cmask[:, :], in_=cmask[:, :], compare_op=ALU.is_ge, fill=MASKED, base=0,
                               pattern=[[-1, P]], channel_multiplier=1).then_inc(consts, 1)
            pool.tensor_copy(slot1[:, :], slot1i[:, :]).then_inc(consts, 1)
            pool.wait_ge(consts, CONSTS - 2)
            pool.memset(plus1[0:64, 0:1], 0.0).then_inc(consts, 1)
            pool.wait_ge(consts, CONSTS - 1)
            pool.memset(plus1[64:P, 1:2], 0.0).then_inc(consts, 1)
            pool.wait_ge(spread_used, SPREADS0)
            for r, w in enumerate((ln_mix_g, ln_mix_b, ln_ffn_g, ln_ffn_b)):
                pool.dma_start(lnrows[32 * r:32 * r + 1, :], w[1:2, :]).then_inc(rows_in[1], 16)


        @block.scalar
        def _(act):
            for t in range(TT):
                act.dma_start(xs[:, t, :], x[0, t * P:(t + 1) * P, :]).then_inc(x_in, 16)
            act.dma_start(colrows[0:TAPS, :], w_dw[0, :, 0, :]).then_inc(small_in, 16)
            act.dma_start(colrows[ROW_BA:ROW_BB + 1, :], b_pw1.rearrange("o (r d) -> (o r) d", r=2)).then_inc(small_in, 16)
            act.dma_start(colrows[ROW_BDW:ROW_BDW + 1, :], b_dw).then_inc(small_in, 16)
            act.dma_start(colrows[ROW_LNG:ROW_LNG + 1, :], conv_ln_g).then_inc(small_in, 16)
            act.dma_start(colrows[ROW_LNB:ROW_LNB + 1, :], conv_ln_b).then_inc(small_in, 16)
            act.dma_start(colrows[ROW_C:ROW_C + 1, :], c).then_inc(small_in, 16)
            for q in range(4):
                for l in range(DEPTH):
                    src = b_ada[l].rearrange("(g q n) -> q g n", g=3, q=4)[q:q + 1]
                    act.dma_start(modv[l][32 * q:32 * q + 32, :, :], src.to_broadcast([32, 3, BANK])).then_inc(small_in, 16)
                src = b_ada_kv.rearrange("(g q n) -> q g n", g=1, q=4)[q:q + 1]
                act.dma_start(modkv[32 * q:32 * q + 32, :, :], src.to_broadcast([32, 1, BANK])).then_inc(small_in, 16)
            act.dma_start(brow[0:1, :], b_pw2).then_inc(small_in, 16)
            act.dma_start(rw[:, :, :], router_w.rearrange("(k p) e -> p k e", p=P)).then_inc(small_in, 16)
            act.dma_start(rbias[:, :], router_b.rearrange("(o e) -> o e", o=1).to_broadcast([P, E])).then_inc(small_in, 16)
            for r, w in enumerate((ln_mix_g, ln_mix_b, ln_ffn_g, ln_ffn_b)):
                act.dma_start(lnrows[32 * r:32 * r + 1, :], w[0:1, :]).then_inc(rows_in[0], 16)
            with nc.allow_non_contiguous_dma(reason="small"):
                act.dma_start(wf[:, :, :], w_kvf[:, 2 * D:2 * D + HEADS].rearrange("(k p) e -> p k e", p=P)).then_inc(small_in, 16)
                act.dma_start(bf[:, :], b_f.rearrange("(h o) -> h o", o=1)).then_inc(small_in, 16)
            act.wait_ge(consts, CONSTS)
            act.wait_ge(cols_copied, 1)
            act.activation(cact[:, :], colv[:, :, ROW_C], ACT.Silu).then_inc(c_acted, 1)

            turned = [0]

            def copy_hT():
                for b in (0, 2):
                    act.wait_ge(h_turned, 4 * turned[0] + b + 1)
                    act.activation(hT[:, 2 * b:2 * b + 2, :], PS[:, b, :].rearrange("p (k t) -> p k t", k=2),
                                   ACT.Copy).then_inc(hT_copied, 1)
                turned[0] += 1

            norms = [0]

            def layer_norm_root():
                act.wait_ge(y_ready, norms[0] // TT + 1)
                for t in range(TT):
                    act.activation(hs[:, t, :], PS[:, 2 * t:2 * t + 2, :].rearrange("p b n -> p (b n)"),
                                   ACT.Copy).then_inc(y_read, 1)
                for t in range(TT):
                    act.wait_ge(ln_var, norms[0] + 1)
                    act.activation(rstd[:, t:t + 1], mv[:, t, 1:2], ACT.Sqrt, bias=eps[:, 0:1]).then_inc(ln_sd, 1)
                    norms[0] += 1

            def moe(l):
                act.wait_ge(lmax_ready, l + 1)
                act.activation(r_ex[:, :, :], r_ex[:, :, :], ACT.Exp).then_inc(lexp_ready, 1)

                def block_of_slots():
                    q1 = act.snap(n_act) + 1
                    act.wait_ge(X_summed, q1)
                    act.activation(Xg, PS[:, B_M, :], ACT.Copy).then_inc(X_copied, 1)
                    act.wait_ge(gate_done, q1)
                    act.activation(sil, PS[:, B_GATE, :], ACT.Silu).then_inc(sil_ready, 1)
                    act.wait_ge(hh_turned, q1)
                    act.activation(hhT.rearrange("p c s -> p (c s)"), PS[:, B_M, :], ACT.Copy).then_inc(hhT_copied, 1)
                    act.wait_ge(down_done, q1)
                    act.activation(yb, PS[:, B_Y, :], ACT.Copy).then_inc(yb_copied, 1)
                    act.reg_add(n_act, n_act, 1)

                act.wait_ge(routed, l + 1)
                with act.Fori(0, E) as e:
                    blocks = act.value_load(blocks_i[0:1, bass.ds(e, 1)], min_val=1, max_val=SEQ // SLOTS)
                    with act.If(blocks > 1):
                        with act.Fori(0, blocks - 1):
                            block_of_slots()
                    block_of_slots()

            n_act = ctx.enter_context(act.register("blocks_act"))
            act.reg_mov(n_act, 0)
            copy_hT()
            for f in range(KD):
                act.wait_ge(u_mm, 1)
                if f >= 2:
                    act.wait_ge(u_ready, f - 1)
                act.activation(SG[:, f % 2, :], PS[:, f, SEQ:2 * SEQ], ACT.Sigmoid,
                               bias=colv[:, f, ROW_BB:ROW_BB + 1]).then_inc(sig_ready, 1)
            act.wait_ge(cen_ready, 1)
            act.activation(hflat, CV.rearrange("p k t -> p (k t)"), ACT.Square).then_inc(sq_ready, 1)
            act.wait_ge(var_done, 1)
            act.activation(crstd, PS[:, 5, 0:SEQ], ACT.Sqrt, bias=eps[:, 0:1]).then_inc(csd_ready, 1)
            act.wait_ge(cnorm_ready, 1)
            for k in range(KD):
                last = act.activation(hT[:, k, :], CV[:, k, :], ACT.Silu, bias=colv[:, k, ROW_LNB:ROW_LNB + 1],
                                      scale=colv[:, k, ROW_LNG:ROW_LNG + 1])
            last.then_inc(z_ready, 1)
            layer_norm_root()
            copy_hT()
            moe(0)
            layer_norm_root()
            copy_hT()
            for b in range(4):
                act.wait_ge(k_done, 1)
                act.activation(KT[:, 2 * b:2 * b + 2, :], PS[:, 4 + b, :].rearrange("p (k t) -> p k t", k=2),
                               ACT.Copy).then_inc(k_copied, 1)
            act.wait_ge(fz_ready, 1)
            act.activation(fe[0:HEADS, :], fe[0:HEADS, :], ACT.Exp, scale=-1.0).then_inc(fe_ready, 1)
            act.wait_ge(fe_ready, 1)
            act.activation(fe[0:HEADS, :], fe[0:HEADS, :], ACT.Ln, bias=ones[0:HEADS, 0:1]).then_inc(fln_ready, 1)
            copy_hT()
            for b in range(4):
                act.wait_ge(q_done, 1)
                act.activation(QT[:, 2 * b:2 * b + 2, :], PS[:, 4 + b, :].rearrange("p (k t) -> p k t", k=2),
                               ACT.Copy, scale=float(HD) ** -0.5).then_inc(q_copied, 1)

            def probs(h):
                act.wait_ge(nmax_ready, h + 1)
                act.activation(PR[:, h % 2, 0:P], PS[:, 4 + h % 2, 0:P], ACT.Exp, bias=nmax[:, 0, h:h + 1],
                               accum_out=rsum[:, 0, h:h + 1])
                act.activation(PR[:, h % 2, P:3 * P], PS[:, 4 + h % 2, P:3 * P], ACT.Exp,
                               bias=nmax[:, 1, h:h + 1], accum_out=rsum[:, 1, h:h + 1]).then_inc(exp_done, 1)

            def take_o(h):
                act.wait_ge(o_done, h + 1)
                r = HD * (h % 2)
                act.activation(hT[r:r + HD, h // 2, :], PS[r:r + HD, h % 2, 0:SEQ], ACT.Copy).then_inc(o_copied, 1)

            for i in range(HEADS + 2):
                if i < HEADS:
                    probs(i)
                if i >= 2:
                    take_o(i - 2)
            layer_norm_root()
            copy_hT()
            moe(1)
            layer_norm_root()
            act.wait_ge(x_done, 1)
            for t in range(TT):
                act.dma_start(out[0, t * P:(t + 1) * P, :], xs[:, t, :]).then_inc(out_done, 16)
            act.wait_ge(out_done, 16 * TT)

        @block.tensor
        def _(pe):
            def quarter(index, k, n):
                return ring[:, index % RING, :].rearrange("p (k f) -> p k f", k=n)[:, k, :]

            def arrived(index, turn=None):
                rounds = index // RING
                if turn is None:
                    pe.wait_ge(landed[index % RING], 16 * (rounds + 1))
                else:
                    pe.wait_ge(landed[index % RING], turn * (16 * TURN // RING) + 16 * (rounds + 1))

            owed = [0]

            def behind(ins):
                if owed[0]:
                    ins.then_inc(half_free, owed[0])
                    owed[0] = 0

            def ada(index, bank):
                for j in range(ADA_G):
                    arrived(index + j)
                    for kk in range(2):
                        k = 2 * j + kk
                        for q in range(4):
                            last = pe.matmul(PS[32 * q:32 * q + 32, bank, :], crep[:, k, :],
                                             quarter(index + j, kk, 2)[:, q * BANK:(q + 1) * BANK],
                                             start=(k == 0), stop=(k == KD - 1), tile_position=(0, 32 * q))
                            if k == 0 and q == 0:
                                behind(last)
                    if j < ADA_G - 1:
                        last.then_inc(half_free, 1)
                last.then_inc(ada_done, 1)
                owed[0] = 1

            spreads = [0]

            def spread_row(row, col=None):
                n = spreads[0]
                if n >= 2:
                    pe.wait_ge(spread_used, n - 1)
                for i in range(2):
                    r, v = row(i)
                    last = pe.matmul(PS[:, 4 + 2 * (n % 2) + i, :], ones[r:r + 1, :], v, start=True, stop=True)
                    if i == 0:
                        behind(last)
                last.then_inc(spread, 1)
                spreads[0] += 1

            def spread_mod(tile, v):
                def row(i):
                    q = 2 * (v % 2) + i
                    return 32 * q, tile[32 * q:32 * q + 1, v // 2, :]
                spread_row(row)

            def spread_ln(r):
                spread_row(lambda i: (32 * r, lnrows[32 * r:32 * r + 1, i * BANK:(i + 1) * BANK]))

            hs_turned = [0]

            def turn_h():
                n = hs_turned[0]
                pe.wait_ge(h_ready, 2 * n + 2)
                for b in range(4):
                    for k in (2 * b, 2 * b + 1):
                        for t in range(TT):
                            last = pe.transpose(PS[:, b, (k % 2) * SEQ + t * P:(k % 2) * SEQ + (t + 1) * P],
                                                hs[:, t, k * P:(k + 1) * P], ident[:, :])
                    last.then_inc(h_turned, 1)
                hs_turned[0] += 1
                pe.wait_ge(hT_copied, 4 * (n + 1))

            def project(index, banks, done=None):
                for h in range(2):
                    arrived(index + h)
                    for kk in range(KH):
                        k = KH * h + kk
                        for t in range(TT):
                            for q in range(2):
                                last = pe.matmul(PS[:, banks + 2 * t + q, :], hT[:, k, t * P:(t + 1) * P],
                                                 quarter(index + h, kk, KH)[:, q * BANK:(q + 1) * BANK],
                                                 start=(k == 0), stop=(k == KD - 1 and done is not None))
                                if k == t == q == 0:
                                    behind(last)
                    if h == 0 or done is None:
                        last.then_inc(half_free, 1)
                if done is not None:
                    last.then_inc(done, 1)
                    owed[0] = 1

            def project_T(index, banks, done):
                for h in range(2):
                    arrived(index + h)
                    for kk in range(KH):
                        k = KH * h + kk
                        for f in range(KD):
                            last = pe.matmul(PS[:, banks + f // 2, (f % 2) * SEQ:(f % 2 + 1) * SEQ],
                                             quarter(index + h, kk, KH)[:, f * P:(f + 1) * P], hT[:, k, :],
                                             start=(k == 0 and f % 2 == 0), stop=(k == KD - 1),
                                             skip_group_check=True)
                            if k == f == 0:
                                behind(last)
                    if h == 0:
                        last.then_inc(half_free, 1)
                last.then_inc(done, 1)
                owed[0] = 1

            def norm_spreads(l, which):
                spread_mod(modv[l], (2, 5)[which])
                pe.wait_ge(rows_in[l], ROWS)
                spread_ln(2 * which)
                spread_ln(2 * which + 1)

            def moe(index, l):
                for t in range(TT):
                    for k in range(KD):
                        last = pe.matmul(PS[:, B_GATE, t * E:(t + 1) * E], hT[:, k, t * P:(t + 1) * P],
                                         rw[:, k, :], start=(k == 0), stop=(k == KD - 1))
                last.then_inc(logits_done, 1)
                for b in range(4):
                    pe.matmul(PS[:, b, :], ident[0:1, 1:2].to_broadcast([1, P]), hs[0:1, 0, 0:BANK],
                              start=True, stop=False, skip_group_check=True)
                pe.wait_ge(sel_ready, l + 1)
                pe.matmul(PS[:, B_UP, 0:E], before[:, :], r_sel[:, 0, :], start=True, stop=True)
                pe.matmul(PS[:, B_UP, E:2 * E], ones[:, :], r_sel[:, 0, :], start=True, stop=False)
                pe.matmul(PS[:, B_UP, E:2 * E], before[:, :], r_sel[:, 1, :], start=False, stop=True)
                pe.matmul(PS[0:1, B_M, 0:E], ones[:, 0:1], r_sel[:, 0, :], start=True, stop=False)
                pe.matmul(PS[0:1, B_M, 0:E], ones[:, 0:1], r_sel[:, 1, :], start=False,
                          stop=True).then_inc(pos_done, 1)

                def block_of_slots(index, turn, final):
                    q1 = pe.snap(n_pe) + 1
                    pe.wait_ge(G_built, q1)
                    for t in range(TT):
                        for q in range(2):
                            last = pe.matmul(PS[SLOTS * q:SLOTS * (q + 1), B_M, :], G[:, t, :],
                                             hs[:, t, q * BANK:(q + 1) * BANK], start=(t == 0),
                                             stop=(t == TT - 1), tile_position=(0, SLOTS * q),
                                             skip_group_check=True)
                    last.then_inc(X_summed, 1)
                    pe.wait_ge(X_copied, q1)
                    for cc in range(KH):
                        last = pe.transpose(PS[:, B_Y, cc * P:(cc + 1) * P], Xg[:, cc * P:(cc + 1) * P], ident[:, :])
                    last.then_inc(X_turned, 1)
                    pe.wait_ge(XT_copied, q1)

                    def product(m, bank, stationary, done, free_previous):
                        for h in range(2):
                            arrived(index + 2 * m + h, turn)
                            for kk in range(KH):
                                for q in range(2):
                                    last = pe.matmul(PS[SLOTS * q:SLOTS * (q + 1), bank, :],
                                                     stationary[:, kk, SLOTS * h:SLOTS * (h + 1)],
                                                     quarter(index + 2 * m + h, kk, KH)[:, q * BANK:(q + 1) * BANK],
                                                     start=(h == 0 and kk == 0), stop=(h == 1 and kk == KH - 1),
                                                     tile_position=(0, SLOTS * q), skip_group_check=True)
                                    if free_previous and h == kk == q == 0:
                                        last.then_inc(half_free, 1)
                            if final and h == 0:
                                last.then_inc(half_free, 1)
                        last.then_inc(done, 1)

                    product(0, B_GATE, XT, gate_done, False)
                    product(1, B_UP, XT, up_done, final)
                    pe.wait_ge(hh_ready, q1)
                    for cc in range(KH):
                        last = pe.transpose(PS[:, B_M, cc * P:(cc + 1) * P], hh[:, cc * P:(cc + 1) * P], ident[:, :])
                        if final and cc == 0:
                            last.then_inc(half_free, 1)
                    last.then_inc(hh_turned, 1)
                    for t in range(TT):
                        last = pe.transpose(PS[:, B_GATE, t * P:(t + 1) * P],
                                            GW[:, t, :, :].rearrange("p q s -> p (q s)"), ident[:, :])
                    last.then_inc(GW_turned, 1)
                    pe.wait_ge(hhT_copied, q1)
                    product(2, B_Y, hhT, down_done, False)
                    pe.wait_ge(GWT_copied, q1)
                    pe.wait_ge(yb_copied, q1)
                    for t in range(TT):
                        for q in range(2):
                            last = pe.matmul(PS[:, 2 * t + q, :], GWT[SLOTS * q:SLOTS * (q + 1), t * P:(t + 1) * P],
                                             yb[SLOTS * q:SLOTS * (q + 1), :], start=False, stop=False,
                                             skip_group_check=True)
                            if final and t == q == 0:
                                last.then_inc(half_free, 1)
                    pe.reg_add(n_pe, n_pe, 1)

                pe.wait_ge(routed, l + 1)
                with pe.Fori(0, E // UNROLL) as turn:
                    for i in range(UNROLL):
                        blocks = pe.value_load(blocks_i[0:1, bass.ds(turn * UNROLL + i, 1)], min_val=1,
                                               max_val=SEQ // SLOTS)
                        with pe.If(blocks > 1):
                            with pe.Fori(0, blocks - 1):
                                block_of_slots(index + 6 * i, turn, False)
                        block_of_slots(index + 6 * i, turn, True)
                for b in range(4):
                    last = pe.matmul(PS[:, b, :], ident[0:1, 1:2].to_broadcast([1, P]), hs[0:1, 0, 0:BANK],
                                     start=False, stop=True, skip_group_check=True)
                last.then_inc(y_ready, 1)

            n_pe = ctx.enter_context(pe.register("blocks_pe"))
            pe.reg_mov(n_pe, 0)
            pe.wait_ge(consts, CONSTS)
            pe.wait_ge(small_in, SMALL)
            for k in range(KD):
                last = pe.transpose(PS[:, B_Y, k * 40:k * 40 + NROWS], colrows[0:NROWS, k * P:(k + 1) * P],
                                    ident[0:NROWS, 0:NROWS])
            last.then_inc(cols_turned, 1)
            pe.wait_ge(c_spread, 1)
            ada(L_ADA0_G0, 0)
            pe.wait_ge(ada_added, 1)
            spread_mod(modv[0], 1)
            spread_mod(modv[0], 0)
            turn_h()
            for j in range(4):
                arrived(L_PW1 + j)
                for kk in range(2):
                    k = 2 * j + kk
                    for f in range(KD):
                        for g in range(2):
                            last = pe.matmul(PS[:, f, g * SEQ:(g + 1) * SEQ],
                                             quarter(L_PW1 + j, kk, 2)[:, g * D + f * P:g * D + (f + 1) * P],
                                             hT[:, k, :], start=(k == 0 and g == 0), stop=(k == KD - 1),
                                             skip_group_check=True)
                if j < 3:
                    last.then_inc(half_free, 1)
            last.then_inc(u_mm, 1)
            pe.wait_ge(sig_ready, 1)
            pe.sem_inc(half_free, 1)
            pe.wait_ge(u_ready, KD)
            ada(L_ADA0_G1, 6)
            ada(L_ADA0_G2, 7)
            pe.wait_ge(conv_ready, KD)
            for k in range(KD):
                last = pe.matmul(PS[:, 4, 0:SEQ], ones_d[:, :], CV[:, k, :], start=(k == 0), stop=(k == KD - 1))
                if k == 0:
                    behind(last)
            last.then_inc(mean_done, 1)
            pe.wait_ge(sq_ready, 1)
            for k in range(KD):
                last = pe.matmul(PS[:, 5, 0:SEQ], ones_d[:, :], hflat[:, k * SEQ:(k + 1) * SEQ],
                                 start=(k == 0), stop=(k == KD - 1))
            last.then_inc(var_done, 1)
            pe.wait_ge(z_ready, 1)
            pe.wait_ge(ada_added, 3)
            project(L_PW2, 0)
            for t in range(TT):
                for q in range(2):
                    last = pe.matmul(PS[:, 2 * t + q, :], ones[0:1, :], brow[0:1, q * BANK:(q + 1) * BANK],
                                     start=False, stop=True)
            last.then_inc(y_ready, 1)
            norm_spreads(0, 0)
            spread_mod(modv[0], 4)
            spread_mod(modv[0], 3)
            turn_h()
            moe(L_MOE0, 0)
            norm_spreads(0, 1)
            pe.wait_ge(y_read, 4)
            ada(L_ADAKV, 0)
            ada(L_ADA1_G0, 1)
            pe.wait_ge(ada_added, 5)
            spread_mod(modkv, 1)
            spread_mod(modkv, 0)
            turn_h()
            project_T(L_WK, 4, k_done)
            project(L_WV, 0, v_done)
            pe.wait_ge(k_copied, 4)
            for k in range(KD):
                last = pe.matmul(PS[0:HEADS, 4, 0:SEQ], wf[:, k, :], hT[:, k, :], start=(k == 0), stop=(k == KD - 1))
                if k == 0:
                    behind(last)
            last.then_inc(f_done, 1)
            pe.wait_ge(v_copied, 4)
            pe.wait_ge(fz_ready, 1)
            spread_mod(modv[1], 1)
            spread_mod(modv[1], 0)
            turn_h()
            pe.wait_ge(logf_ready, 1)
            project_T(L_WQ, 4, q_done)
            for t in range(TT):
                last = pe.transpose(PS[:, 0, t * HEADS:(t + 1) * HEADS], fl[0:HEADS, t * P:(t + 1) * P],
                                    ident[0:HEADS, 0:HEADS])
                if t == 0:
                    behind(last)
            last.then_inc(logf_turned, 1)
            pe.wait_ge(ltok_copied, 1)
            pe.matmul(PS[:, 1, 0:HEADS], upto[:, :], ltok[:, 0, :], start=True, stop=True)
            pe.matmul(PS[:, 1, HEADS:2 * HEADS], ones[:, :], ltok[:, 0, :], start=True, stop=False)
            pe.matmul(PS[:, 1, HEADS:2 * HEADS], upto[:, :], ltok[:, 1, :], start=False, stop=True)
            pe.matmul(PS[0:HEADS, 2, 0:P], ltok[:, 0, :], upto[:, :], start=True, stop=True)
            pe.matmul(PS[0:HEADS, 2, P:2 * P], ltok[:, 0, :], ones[:, :], start=True, stop=False)
            pe.matmul(PS[0:HEADS, 2, P:2 * P], ltok[:, 1, :], upto[:, :], start=False, stop=True).then_inc(fcum_done, 1)
            pe.wait_ge(fcum_copied, 1)
            pe.wait_ge(q_copied, 4)

            def scores(h):
                b, r, hp = 4 + h % 2, HD * (h % 2), h // 2
                one_h = ident[0:HEADS, h:h + 1].to_broadcast([HEADS, P])
                for t in range(TT):
                    o, n = (0, P, 3 * P)[t], (t + 1) * P
                    pe.matmul(PS[:, b, o:o + n], QT[r:r + HD, hp, t * P:(t + 1) * P], KT[r:r + HD, hp, 0:n],
                              start=True, stop=False, skip_group_check=True)
                    pe.matmul(PS[:, b, o:o + n], one_h, nfc[0:HEADS, 0:n], start=False, stop=False,
                              skip_group_check=True)
                    last = pe.matmul(PS[:, b, o + n - P:o + n], ident[:, :], cmask[:, :], start=False, stop=True,
                                     skip_group_check=True)
                last.then_inc(s_done, 1)

            def turn_probs(h):
                pe.wait_ge(p_ready, h + 1)
                for i in range(3):
                    last = pe.transpose(PS[:, 2 + h % 2, i * P:(i + 1) * P], PR[:, h % 2, i * P:(i + 1) * P], ident[:, :])
                last.then_inc(p_turned, 1)

            def weigh(h):
                pe.wait_ge(pT_copied, h + 1)
                if h >= 2:
                    pe.wait_ge(o_copied, h - 1)
                r = HD * (h % 2)
                o = PS[r:r + HD, h % 2, :]
                v = V[:, :, h * HD:(h + 1) * HD]
                pe.matmul(o[:, 0:P], v[:, 0, :], PRT[:, h % 2, 0:P], start=True, stop=True)
                pe.matmul(o[:, P:2 * P], v[:, 0, :], PRT[:, h % 2, P:2 * P], start=True, stop=False)
                pe.matmul(o[:, P:2 * P], v[:, 1, :], PRT[:, h % 2, 2 * P:3 * P], start=False,
                          stop=True).then_inc(o_done, 1)

            for i in range(HEADS + 2):
                if i < HEADS:
                    scores(i)
                if 1 <= i <= HEADS:
                    turn_probs(i - 1)
                if i >= 2:
                    weigh(i - 2)
            ada(L_ADA1_G1, 6)
            ada(L_ADA1_G2, 7)
            pe.wait_ge(o_copied, HEADS)
            project(L_WO, 0, y_ready)
            pe.wait_ge(ada_added, 7)
            norm_spreads(1, 0)
            spread_mod(modv[1], 4)
            spread_mod(modv[1], 3)
            turn_h()
            moe(L_MOE1, 1)
            norm_spreads(1, 1)

        @block.vector
        def _(dve):
            chain = [0]

            def link(ins):
                chain[0] += 1
                ins.then_inc(dchain, 1)
                dve.wait_ge(dchain, chain[0])

            turned, adas, spreads, norms, ys = [0], [0], [0], [0], [0]

            def copy_hT():
                for b in (1, 3):
                    dve.wait_ge(h_turned, 4 * turned[0] + b + 1)
                    dve.tensor_copy(hT[:, 2 * b:2 * b + 2, :],
                                    PS[:, b, :].rearrange("p (k t) -> p k t", k=2)).then_inc(hT_copied, 1)
                turned[0] += 1

            def add_ada(tile, g, bank):
                adas[0] += 1
                dve.wait_ge(ada_done, adas[0])
                dve.scalar_tensor_tensor(out=tile[:, g, :], in0=tile[:, g, :], scalar=plus1[:, g:g + 1],
                                         in1=PS[:, bank, :], op0=ALU.add, op1=ALU.add).then_inc(ada_added, 1)

            def spread_banks():
                n = spreads[0]
                dve.wait_ge(spread, n + 1)
                spreads[0] += 1
                b = 4 + 2 * (n % 2)
                return PS[:, b:b + 2, :].rearrange("p b n -> p (b n)")

            def with_row(dst, src, op):
                row = spread_banks()
                for t in range(TT):
                    last = dve.tensor_tensor(dst[:, t, :], src[:, t, :], row, op)
                last.then_inc(spread_used, 1)
                dve.wait_ge(spread_used, spreads[0])

            def modulate():
                with_row(hs, xs, ALU.mult)
                row = spread_banks()
                for t in range(TT):
                    dve.tensor_tensor(hs[:, t, :], hs[:, t, :], row, ALU.add).then_inc(h_ready, 1)
                hn[0] += 2
                dve.wait_ge(h_ready, hn[0])
                dve.sem_inc(spread_used, 1)

            hn = [0]

            def close_sublayer():
                ys[0] += 1
                row = spread_banks()
                for t in range(TT):
                    dve.wait_ge(y_read, 2 * (ys[0] - 1) + t + 1)
                    last = dve.tensor_tensor(hs[:, t, :], hs[:, t, :], row, ALU.mult)
                last.then_inc(spread_used, 1)
                dve.wait_ge(spread_used, spreads[0])
                for t in range(TT):
                    last = dve.scalar_tensor_tensor(out=xs[:, t, :], in0=xs[:, t, :], scalar=ALPHA, in1=hs[:, t, :],
                                                    op0=ALU.mult, op1=ALU.add)
                link(last)
                for t in range(TT):
                    for q in range(2):
                        last = dve.bn_stats(stats[:, t, q, :], xs[:, t, q * BANK:(q + 1) * BANK])
                link(last)
                for t in range(TT):
                    dve.bn_aggr(mv[:, t, :], stats[:, t, :, :].rearrange("p q s -> p (q s)")).then_inc(ln_var, 1)
                norms[0] += 2
                dve.wait_ge(ln_sd, norms[0])
                link(dve.reciprocal(rstd[:, :], rstd[:, :]))
                for t in range(TT):
                    last = dve.tensor_scalar(xs[:, t, :], xs[:, t, :], mv[:, t, 0:1], rstd[:, t:t + 1],
                                             ALU.subtract, ALU.mult)
                link(last)
                with_row(xs, xs, ALU.mult)
                with_row(xs, xs, ALU.add)

            def ranks(rank, compared, values, n):
                for d in range(1, n):
                    link(dve.tensor_tensor(compared[:, :, 0:n - d], values[:, :, 0:n - d], values[:, :, d:n], ALU.is_ge))
                    link(dve.tensor_tensor(rank[:, :, d:n], rank[:, :, d:n], compared[:, :, 0:n - d], ALU.add))
                    link(dve.tensor_tensor(rank[:, :, 0:n - d], rank[:, :, 0:n - d], compared[:, :, 0:n - d], ALU.subtract))

            def moe(l):
                lg = PS[:, B_GATE, 0:TT * E].rearrange("p (t e) -> p t e", t=TT)
                dve.wait_ge(logits_done, l + 1)
                link(dve.tensor_tensor(r_p[:, :, :], lg, rbias[:, :].unsqueeze(1).to_broadcast([P, TT, E]), ALU.add))
                link(dve.tensor_reduce(r_s[:, :], r_p[:, :, :], AX.X, ALU.max))
                dve.tensor_tensor(r_ex[:, :, :], r_p[:, :, :], r_s[:, :].unsqueeze(2).to_broadcast([P, TT, E]),
                                  ALU.subtract).then_inc(lmax_ready, 1)
                dve.wait_ge(lexp_ready, l + 1)
                link(dve.tensor_reduce(r_s[:, :], r_ex[:, :, :], AX.X, ALU.add))
                link(dve.reciprocal(r_s[:, :], r_s[:, :]))
                link(dve.tensor_tensor(r_p[:, :, :], r_ex[:, :, :], r_s[:, :].unsqueeze(2).to_broadcast([P, TT, E]), ALU.mult))
                pg = r_p[:, :, :].rearrange("p t (g i) -> p (t g) i", g=GROUPS)
                selg = r_sel[:, :, :].rearrange("p t (g i) -> p (t g) i", g=GROUPS)
                wg = r_w[:, :, :].rearrange("p t (g i) -> p (t g) i", g=GROUPS)
                link(dve.tensor_copy(r_rk[:, :, :], later[:, :, :]))
                ranks(r_rk, r_c, pg, PER)
                link(dve.tensor_scalar(selg, r_rk[:, :, :], 2.0, None, ALU.is_lt))
                link(dve.tensor_tensor(wg, pg, selg, ALU.mult))
                link(dve.tensor_reduce(r_gs[:, :, :].rearrange("p t g -> p (t g)"), wg, AX.X, ALU.add))
                link(dve.tensor_copy(r_gr[:, :, :], later[:, 0:TT, :]))
                ranks(r_gr, r_gc, r_gs, GROUPS)
                link(dve.tensor_scalar(r_gs[:, :, :], r_gr[:, :, :], 1.0, None, ALU.is_lt))
                gb = r_gs[:, :, :].rearrange("p t g -> p (t g)").unsqueeze(2).to_broadcast([P, 2 * GROUPS, PER])
                dve.tensor_tensor(selg, selg, gb, ALU.mult).then_inc(sel_ready, 1)
                link(dve.tensor_tensor(wg, wg, gb, ALU.mult))
                link(dve.tensor_reduce(r_s[:, :], r_w[:, :, :], AX.X, ALU.add))
                link(dve.reciprocal(r_s[:, :], r_s[:, :]))
                link(dve.tensor_tensor(r_w[:, :, :], r_w[:, :, :], r_s[:, :].unsqueeze(2).to_broadcast([P, TT, E]), ALU.mult))
                dve.wait_ge(pos_done, l + 1)
                dve.wait_ge(sel_ready, l + 1)
                link(dve.scalar_tensor_tensor(out=r_pos[:, :, :],
                                              in0=PS[:, B_UP, 0:TT * E].rearrange("p (t e) -> p t e", t=TT),
                                              scalar=1.0, in1=r_sel[:, :, :], op0=ALU.add, op1=ALU.mult))
                cnt = PS[0:1, B_M, 0:E]
                link(dve.tensor_scalar(r_n[:, :], cnt, float(SLOTS), 1.0, ALU.is_gt, ALU.add))
                for m in range(2, SEQ // SLOTS):
                    dst = r_n if m < SEQ // SLOTS - 1 else blocks_i
                    link(dve.scalar_tensor_tensor(out=dst[:, :], in0=cnt, scalar=float(m * SLOTS), in1=r_n[:, :],
                                                  op0=ALU.is_gt, op1=ALU.add))
                dve.sem_inc(routed, 1)

                def block_of_slots(e, first_slot):
                    q1 = dve.snap(n_dve) + 1
                    slots = slot1[:, bass.ds(first_slot, SLOTS)]
                    for t in range(TT):
                        dve.tensor_scalar(G[:, t, :], slots, r_pos[:, t, bass.ds(e, 1)], None, ALU.is_equal)
                    for t in range(TT):
                        for q in range(2):
                            last = dve.tensor_scalar(GW[:, t, q, :], slots, r_pos[:, t, bass.ds(e, 1)],
                                                     r_w[:, t, bass.ds(e, 1)], ALU.is_equal, ALU.mult)
                    last.then_inc(G_built, 1)
                    dve.wait_ge(X_turned, q1)
                    dve.tensor_copy(XT.rearrange("p c s -> p (c s)"), PS[:, B_Y, :]).then_inc(XT_copied, 1)
                    dve.wait_ge(sil_ready, q1)
                    dve.wait_ge(up_done, q1)
                    dve.tensor_tensor(hh, sil, PS[:, B_UP, :], ALU.mult).then_inc(hh_ready, 1)
                    dve.wait_ge(GW_turned, q1)
                    dve.tensor_copy(GWT, PS[:, B_GATE, 0:SEQ]).then_inc(GWT_copied, 1)
                    dve.reg_add(n_dve, n_dve, 1)

                dve.wait_ge(routed, l + 1)
                with dve.Fori(0, E) as e:
                    blocks = dve.value_load(blocks_i[0:1, bass.ds(e, 1)], min_val=1, max_val=SEQ // SLOTS)
                    with dve.If(blocks > 1):
                        with dve.Fori(0, blocks - 1) as j:
                            block_of_slots(e, j * SLOTS)
                    block_of_slots(e, (blocks - 1) * SLOTS)

            n_dve = ctx.enter_context(dve.register("blocks_dve"))
            dve.reg_mov(n_dve, 0)
            link(dve.memset(U[:, :, 0:PAD], 0.0))
            dve.wait_ge(consts, CONSTS)
            dve.wait_ge(cols_turned, 1)
            dve.tensor_copy(colv[:, :, :], PS[:, B_Y, 0:KD * 40].rearrange("p (k r) -> p k r", r=40)[:, :, 0:NROWS]).then_inc(cols_copied, 1)
            dve.wait_ge(c_acted, 1)
            dve.tensor_copy(crep[:, :, :], cact[:, :].unsqueeze(2).to_broadcast([P, KD, 32])).then_inc(c_spread, 1)
            dve.wait_ge(small_in, SMALL)
            add_ada(modv[0], 0, 0)
            dve.wait_ge(x_in, 16 * TT)
            modulate()
            copy_hT()
            dve.wait_ge(cols_copied, 1)
            for f in range(KD):
                dve.wait_ge(sig_ready, f + 1)
                dve.scalar_tensor_tensor(out=U[:, f, PAD:PAD + SEQ], in0=PS[:, f, 0:SEQ],
                                         scalar=colv[:, f, ROW_BA:ROW_BA + 1], in1=SG[:, f % 2, :],
                                         op0=ALU.add, op1=ALU.mult).then_inc(u_ready, 1)
            dve.wait_ge(u_ready, KD)
            for f in range(KD):
                link(dve.tensor_scalar(CV[:, f, :], U[:, f, 0:SEQ], colv[:, f, 0:1], colv[:, f, ROW_BDW:ROW_BDW + 1],
                                       ALU.mult, ALU.add))
                for j in range(1, TAPS):
                    last = dve.scalar_tensor_tensor(out=CV[:, f, :], in0=U[:, f, j:j + SEQ], scalar=colv[:, f, j:j + 1],
                                                    in1=CV[:, f, :], op0=ALU.mult, op1=ALU.add)
                    if j < TAPS - 1:
                        link(last)
                last.then_inc(conv_ready, 1)
            add_ada(modv[0], 1, 6)
            add_ada(modv[0], 2, 7)
            dve.wait_ge(conv_ready, KD)
            dve.wait_ge(mean_done, 1)
            dve.tensor_tensor(CV, CV, PS[:, 4, 0:SEQ].unsqueeze(1).to_broadcast([P, KD, SEQ]), ALU.subtract).then_inc(cen_ready, 1)
            dve.wait_ge(cen_ready, 1)
            dve.wait_ge(csd_ready, 1)
            link(dve.reciprocal(crstd, crstd))
            dve.tensor_tensor(CV, CV, crstd.unsqueeze(1).to_broadcast([P, KD, SEQ]), ALU.mult).then_inc(cnorm_ready, 1)
            close_sublayer()
            modulate()
            copy_hT()
            moe(0)
            close_sublayer()
            add_ada(modkv, 0, 0)
            add_ada(modv[1], 0, 1)
            modulate()
            copy_hT()
            for t in range(TT):
                for q in range(2):
                    dve.wait_ge(v_done, 1)
                    dve.tensor_copy(V[:, t, q * BANK:(q + 1) * BANK], PS[:, 2 * t + q, :]).then_inc(v_copied, 1)
            dve.wait_ge(f_done, 1)
            link(dve.tensor_scalar(fz[0:HEADS, :], PS[0:HEADS, 4, 0:SEQ], bf[:, 0:1], None, ALU.add))
            link(dve.tensor_scalar(fe[0:HEADS, :], fz[0:HEADS, :], -1.0, None, ALU.mult))
            dve.tensor_tensor(fe[0:HEADS, :], fe[0:HEADS, :], fz[0:HEADS, :], ALU.max).then_inc(fz_ready, 1)
            dve.wait_ge(fln_ready, 1)
            dve.scalar_tensor_tensor(out=fl[0:HEADS, :], in0=fz[0:HEADS, :], scalar=0.0, in1=fe[0:HEADS, :],
                                     op0=ALU.min, op1=ALU.subtract).then_inc(logf_ready, 1)
            modulate()
            copy_hT()
            dve.wait_ge(logf_turned, 1)
            dve.tensor_copy(ltok, PS[:, 0, 0:TT * HEADS].rearrange("p (t h) -> p t h", t=TT)).then_inc(ltok_copied, 1)
            dve.wait_ge(fcum_done, 1)
            dve.tensor_scalar(nfc[0:HEADS, :], PS[0:HEADS, 2, 0:SEQ], -1.0, None, ALU.mult)
            link(dve.tensor_copy(fq, PS[:, 1, 0:TT * HEADS].rearrange("p (t h) -> p t h", t=TT)))
            dve.sem_inc(fcum_copied, 1)

            def row_max(h):
                b = 4 + h % 2
                dve.wait_ge(s_done, h + 1)
                dve.tensor_reduce(rmax[:, 0, h:h + 1], PS[:, b, 0:P], AX.X, ALU.max)
                link(dve.tensor_reduce(rmax[:, 1, h:h + 1], PS[:, b, P:3 * P], AX.X, ALU.max))
                link(dve.tensor_tensor(rmax[:, :, h], rmax[:, :, h], fq[:, :, h], ALU.add))
                dve.tensor_tensor(nmax[:, :, h], fq[:, :, h], rmax[:, :, h], ALU.subtract).then_inc(nmax_ready, 1)

            def normalise(h):
                dve.wait_ge(exp_done, h + 1)
                link(dve.reciprocal(rinv[:, :, h], rsum[:, :, h]))
                dve.tensor_scalar(PR[:, h % 2, 0:P], PR[:, h % 2, 0:P], rinv[:, 0, h:h + 1], None, ALU.mult)
                dve.tensor_scalar(PR[:, h % 2, P:3 * P], PR[:, h % 2, P:3 * P], rinv[:, 1, h:h + 1], None,
                                  ALU.mult).then_inc(p_ready, 1)

            def copy_pT(h):
                dve.wait_ge(p_turned, h + 1)
                dve.tensor_copy(PRT[:, h % 2, :], PS[:, 2 + h % 2, 0:3 * P]).then_inc(pT_copied, 1)

            for i in range(HEADS + 2):
                if i < HEADS:
                    row_max(i)
                if 1 <= i <= HEADS:
                    normalise(i - 1)
                if i >= 2:
                    copy_pT(i - 2)
            add_ada(modv[1], 1, 6)
            add_ada(modv[1], 2, 7)
            close_sublayer()
            modulate()
            copy_hT()
            moe(1)
            close_sublayer()
            dve.sem_inc(x_done, 1)


_INS = ["x", "c", "w_ada", "b_ada", "ln_mix_g", "ln_mix_b", "ln_ffn_g", "ln_ffn_b",
        "w_pw1", "b_pw1", "w_dw", "b_dw", "conv_ln_g", "conv_ln_b", "w_pw2", "b_pw2",
        "w_ada_kv", "b_ada_kv", "w_kvf", "b_f", "w_q", "w_o",
        "router_w", "router_b", "w_gate", "w_up", "w_down"]


def kernel(**inputs):
    import numpy as _np
    import concourse.bacc as _bacc
    from concourse import mybir as _mybir
    from concourse.bass_utils import run_bass_kernel_spmd as _run

    nc = _bacc.Bacc("TRN2", target_bir_lowering=False, num_devices=1)
    arrays, args = {}, []
    for name in _INS:
        a = _np.ascontiguousarray(inputs[name])
        arrays[f"in_{name}_dram"] = a
        args.append(nc.dram_tensor(f"in_{name}_dram", a.shape, _mybir.dt.from_np(a.dtype), kind="ExternalInput").ap())
    shape = arrays["in_x_dram"].shape
    args.append(nc.dram_tensor("out_0_dram", shape, _mybir.dt.float32, kind="ExternalOutput").ap())
    trunk_kernel(nc, *args)
    r = _run(nc, [arrays], core_ids=[0])
    return r.results[0]["out_0_dram"]
```

```python
import math
from contextlib import ExitStack

import concourse.bass as bass
from concourse import mybir

F32 = mybir.dt.float32
I32 = mybir.dt.int32
ALU = mybir.AluOpType
ACT = mybir.ActivationFunctionType
AX = mybir.AxisListType

P = 128
BANK = 512
SLOTS = 64
RING = 8
MASKED = -1e30
LN_EPS = 1e-5


def trunk_kernel(nc, x, c, w_ada, b_ada, ln_mix_g, ln_mix_b, ln_ffn_g, ln_ffn_b,
                 w_pw1, b_pw1, w_dw, b_dw, conv_ln_g, conv_ln_b, w_pw2, b_pw2,
                 w_ada_kv, b_ada_kv, w_kvf, b_f, w_q, w_o,
                 router_w, router_b, w_gate, w_up, w_down, out):
    DEPTH, E, D, F = w_gate.shape
    SEQ = x.shape[1]
    TAPS = w_dw.shape[1]
    HEADS = b_f.shape[0]
    HD = D // HEADS
    GROUPS, PER = 4, 4
    TT = SEQ // P
    KD = D // P
    KH = KD // 2
    HALF = D // 2
    PAD = TAPS - 1
    ALPHA = (2.0 * DEPTH) ** 0.25
    assert (D, F, TT, HD, E, DEPTH) == (1024, 1024, 2, 64, GROUPS * PER, 2)
    assert HALF == BANK and SLOTS * 2 == P

    ROW_BA, ROW_BB, ROW_BDW, ROW_LNG, ROW_LNB, ROW_C = range(TAPS, TAPS + 6)
    NROWS = TAPS + 6

    ADA_G = 4
    L_ADA0_G0 = 0
    L_PW1 = L_ADA0_G0 + ADA_G
    L_ADA0_G1 = L_PW1 + 4
    L_ADA0_G2 = L_ADA0_G1 + ADA_G
    L_PW2 = L_ADA0_G2 + ADA_G
    L_ADAKV = L_PW2 + 2
    L_ADA1_G0 = L_ADAKV + ADA_G
    L_MOE0 = L_ADA1_G0 + ADA_G
    L_ADA1_G1 = L_MOE0 + 6 * E
    L_WK = L_ADA1_G1 + ADA_G
    L_WV = L_WK + 2
    L_WQ = L_WV + 2
    L_ADA1_G2 = L_WQ + 2
    L_WO = L_ADA1_G2 + ADA_G
    L_MOE1 = L_WO + 2
    UNROLL = 4
    TURN = 6 * UNROLL
    assert TURN % RING == 0 and E % UNROLL == 0

    def halves(w, rows_first=0):
        return w.rearrange("(h k p) f -> h p k f", h=2, p=P)

    wide_ada = [[w_ada[l, :, g * 2048:(g + 1) * 2048].rearrange("(j k p) f -> j p k f", k=2, p=P)
                 for g in range(3)] for l in range(DEPTH)]
    wide_kv = w_ada_kv.rearrange("(j k p) f -> j p k f", k=2, p=P)
    wide_pw1 = w_pw1[0].rearrange("(j k p) f -> j p k f", k=2, p=P)
    pw2_h = halves(w_pw2[0])
    wk_h = halves(w_kvf[:, 0:D])
    wv_h = halves(w_kvf[:, D:2 * D])
    wq_h = halves(w_q[0])
    wo_h = halves(w_o[0])
    gate_h = w_gate.rearrange("l e (h k p) f -> (l e) h p k f", h=2, p=P)
    up_h = w_up.rearrange("l e (h k p) f -> (l e) h p k f", h=2, p=P)
    down_h = w_down.rearrange("l e (h k p) f -> (l e) h p k f", h=2, p=P)

    ctx = ExitStack()
    with ctx:
        def sb(name, shape, dt=F32):
            return ctx.enter_context(nc.sbuf_tensor(name, shape, dt))

        def sem(name):
            return ctx.enter_context(nc.semaphore(name))

        ring = sb("ring", [P, RING, KH * D])
        xs = sb("xs", [P, TT, D])
        hs = sb("hs", [P, TT, D])
        hT = sb("hT", [P, KD, SEQ])
        work = sb("work", [P, 7168])
        modv = [sb(f"modv{l}", [P, 3, BANK]) for l in range(DEPTH)]
        modkv = sb("modkv", [P, 1, BANK])
        lnrows = sb("lnrows", [P, D])
        colv = sb("colv", [P, KD, NROWS])
        cact = sb("cact", [P, KD])
        crep = sb("crep", [P, KD, 32])
        rw = sb("rw", [P, KD, E])
        rbias = sb("rbias", [P, E])
        wf = sb("wf", [P, KD, HEADS])
        bf = sb("bf", [HEADS, 1])
        ident = sb("ident", [P, P])
        before = sb("before", [P, P])
        upto = sb("upto", [P, P])
        ones = sb("ones", [P, P])
        ones_d = sb("ones_d", [P, P])
        slot1 = sb("slot1", [P, SEQ + SLOTS])
        cmask = sb("cmask", [P, P])
        plus1 = sb("plus1", [P, 3])
        later = sb("later", [P, 2 * GROUPS, PER])
        eps = sb("eps", [P, 1])
        stats = sb("stats", [P, TT, 2, 6])
        mv = sb("mv", [P, TT, 2])
        rstd = sb("rstd", [P, TT])
        r_ex = sb("r_ex", [P, TT, E])
        r_p = sb("r_p", [P, TT, E])
        r_c = sb("r_c", [P, 2 * GROUPS, PER])
        r_rk = sb("r_rk", [P, 2 * GROUPS, PER])
        r_sel = sb("r_sel", [P, TT, E])
        r_gs = sb("r_gs", [P, TT, GROUPS])
        r_gc = sb("r_gc", [P, TT, GROUPS])
        r_gr = sb("r_gr", [P, TT, GROUPS])
        r_w = sb("r_w", [P, TT, E])
        r_pos = sb("r_pos", [P, TT, E])
        r_s = sb("r_s", [P, TT])
        r_n = sb("r_n", [1, E])
        blocks_i = sb("blocks_i", [1, E], I32)

        at = [0]

        def part(n, **kw):
            a = work[:, at[0]:at[0] + n]
            at[0] += n
            return a.rearrange(kw["to"], **{k: v for k, v in kw.items() if k != "to"}) if kw else a

        Xg = [part(BANK) for _ in range(2)]
        XT = [part(BANK, to="p (c s) -> p c s", c=KH) for _ in range(2)]
        hh = [part(BANK) for _ in range(2)]
        hhT = [part(BANK, to="p (c s) -> p c s", c=KH) for _ in range(2)]
        yb = [part(BANK) for _ in range(2)]
        G = [part(TT * SLOTS, to="p (t s) -> p t s", t=TT) for _ in range(2)]
        GW = [part(TT * P, to="p (t q s) -> p t q s", t=TT, q=2) for _ in range(2)]
        GWT = [part(SEQ) for _ in range(2)]
        at[0] = 0
        U = part(KD * (SEQ + PAD), to="p (k t) -> p k t", k=KD)
        CV = part(KD * SEQ, to="p (k t) -> p k t", k=KD)
        colrows = part(D)
        brow = part(D)
        SG = part(2 * SEQ, to="p (b t) -> p b t", b=2)
        crstd = part(SEQ)
        tap = crstd
        at[0] = 0
        KT = part(KD * SEQ, to="p (k t) -> p k t", k=KD)
        QT = part(KD * SEQ, to="p (k t) -> p k t", k=KD)
        V = part(TT * D, to="p (t d) -> p t d", t=TT)
        fz = part(SEQ)
        fe = part(SEQ)
        fl = part(SEQ)
        nfc = part(SEQ)
        hflat = hs[:, :, :].rearrange("p t d -> p (t d)")
        PR = hflat[:, 0:1152].rearrange("p (b n) -> p b n", b=3)
        PRT = hflat[:, 1152:1920].rearrange("p (b n) -> p b n", b=2)
        at[0] = 3 * KD * SEQ
        ltok, fq, rmax, nmax, rsum, rinv = (part(TT * HEADS, to="p (t h) -> p t h", t=TT) for _ in range(6))

        PS = ctx.enter_context(nc.psum_tensor("PS", [P, 8, BANK], F32))
        B_GATE, B_UP, B_Y, B_M = 4, 5, 6, 7
        X_BANK, XT_BANK = (7, 5), (6, 4)
        GATE_BANK, UP_BANK = (4, 6), (5, 7)
        HT_BANK, GWT_BANK, DOWN_BANK = (4, 6), (5, 7), (5, 7)

        landed = [sem(f"landed{i}") for i in range(RING)]
        half_free = sem("half_free")
        consts = sem("consts")
        colrows_in = sem("colrows_in")
        mod0_in = sem("mod0_in")
        later_in = sem("later_in")
        x_in = sem("x_in")
        rows_in = [sem(f"rows_in{l}") for l in range(DEPTH)]
        x_done = sem("x_done")
        out_done = sem("out_done")
        dchain = sem("dchain")
        cols_turned = sem("cols_turned")
        cols_copied = sem("cols_copied")
        c_acted = sem("c_acted")
        c_spread = sem("c_spread")
        ada_done = sem("ada_done")
        ada_added = sem("ada_added")
        spread = sem("spread")
        spread_used = sem("spread_used")
        h_ready = sem("h_ready")
        h_turned = sem("h_turned")
        hT_copied = sem("hT_copied")
        u_mm = sem("u_mm")
        sig_ready = sem("sig_ready")
        u_ready = sem("u_ready")
        conv_ready = sem("conv_ready")
        diag_ready = sem("diag_ready")
        diag_used = sem("diag_used")
        pchain = sem("pchain")
        mean_done = sem("mean_done")
        cen_ready = sem("cen_ready")
        sq_ready = sem("sq_ready")
        var_done = sem("var_done")
        csd_ready = sem("csd_ready")
        cnorm_ready = sem("cnorm_ready")
        z_ready = sem("z_ready")
        y_ready = sem("y_ready")
        y_read = sem("y_read")
        ln_var = sem("ln_var")
        ln_sd = sem("ln_sd")
        logits_done = sem("logits_done")
        lmax_ready = sem("lmax_ready")
        lexp_ready = sem("lexp_ready")
        sel_ready = sem("sel_ready")
        pos_done = sem("pos_done")
        routed = sem("routed")
        G_built = sem("G_built")
        X_summed = sem("X_summed")
        X_copied = sem("X_copied")
        X_turned = sem("X_turned")
        XT_copied = sem("XT_copied")
        gate_done = sem("gate_done")
        sil_ready = sem("sil_ready")
        up_done = sem("up_done")
        hh_ready = sem("hh_ready")
        hh_turned = sem("hh_turned")
        hhT_copied = sem("hhT_copied")
        GW_turned = sem("GW_turned")
        GWT_copied = sem("GWT_copied")
        down_done = sem("down_done")
        yb_copied = sem("yb_copied")
        k_done = sem("k_done")
        k_copied = sem("k_copied")
        v_done = sem("v_done")
        v_copied = sem("v_copied")
        f_done = sem("f_done")
        fz_ready = sem("fz_ready")
        fe_ready = sem("fe_ready")
        fln_ready = sem("fln_ready")
        logf_ready = sem("logf_ready")
        logf_turned = sem("logf_turned")
        ltok_copied = sem("ltok_copied")
        fcum_done = sem("fcum_done")
        fcum_copied = sem("fcum_copied")
        q_done = sem("q_done")
        q_copied = sem("q_copied")
        s_done = sem("s_done")
        nmax_ready = sem("nmax_ready")
        exp_done = sem("exp_done")
        p_ready = sem("p_ready")
        p_turned = sem("p_turned")
        pT_copied = sem("pT_copied")
        o_done = sem("o_done")
        o_copied = sem("o_copied")

        CONV_PE, CONV_POOL = (6, 7), (0,)
        DVE_STEPS = (("u", 0), ("u", 1), ("u", 2), ("conv", (1, 2), 0, 16), ("u", 3), ("conv", (1, 2), 16, 31),
                     ("u", 4), ("conv", (3, 4), 0, 12), ("u", 5), ("conv", (3, 4), 12, 24), ("u", 6),
                     ("conv", (3, 4), 24, 31), ("u", 7), ("conv", (5,), 0, 31))
        DIAGS = 16

        def diag(n):
            return hs[:, :, :].rearrange("p t d -> p (t d)")[:, (n % DIAGS) * P:(n % DIAGS + 1) * P]

        CONSTS = 17
        COLROWS = 16 * 6
        LATER = 16 * 13
        ROWS = 16 * 4
        SPREADS0 = 10

        block = ctx.enter_context(nc.Block())

        @block.sync
        def _(sp):
            def load(index, source, turn=0):
                if isinstance(turn, int):
                    if index + 1 > RING:
                        sp.wait_ge(half_free, index + 1 - RING)
                else:
                    sp.wait_ge(half_free, turn + (index + 1 - RING))
                n = source.shape[-2]
                sp.dma_start(ring[:, index % RING, :].rearrange("p (k f) -> p k f", k=n),
                             source).then_inc(landed[index % RING], 16)

            def load_wide(index, w):
                for j in range(ADA_G):
                    load(index + j, w[j])

            def load_pair(index, w):
                for h in range(2):
                    load(index + h, w[h])

            def load_experts(index, l):
                with sp.Fori(0, E // UNROLL) as turn:
                    for i in range(UNROLL):
                        e = turn * UNROLL + (l * E + i)
                        for m, w in enumerate((gate_h, up_h, down_h)):
                            for h in range(2):
                                load(index + 6 * i + 2 * m + h,
                                     w[bass.ds(e, 1), h].rearrange("o p k f -> (o p) k f"), turn * TURN)

            for r, w in ((0, w_dw[0, :, 0, :]), (ROW_BA, b_pw1.rearrange("o (r d) -> (o r) d", r=2)), (ROW_BDW, b_dw),
                         (ROW_LNG, conv_ln_g), (ROW_LNB, conv_ln_b), (ROW_C, c)):
                sp.dma_start(colrows[r:r + w.shape[0], :], w).then_inc(colrows_in, 16)
            load_wide(L_ADA0_G0, wide_ada[0][0])
            load_wide(L_PW1, wide_pw1)
            load_wide(L_ADA0_G1, wide_ada[0][1])
            load_wide(L_ADA0_G2, wide_ada[0][2])
            load_pair(L_PW2, pw2_h)
            load_wide(L_ADAKV, wide_kv)
            load_wide(L_ADA1_G0, wide_ada[1][0])
            load_experts(L_MOE0, 0)
            load_wide(L_ADA1_G1, wide_ada[1][1])
            load_pair(L_WK, wk_h)
            load_pair(L_WV, wv_h)
            load_pair(L_WQ, wq_h)
            load_wide(L_ADA1_G2, wide_ada[1][2])
            load_pair(L_WO, wo_h)
            load_experts(L_MOE1, 1)

        @block.gpsimd
        def _(pool):
            pool.memset(ident[:, :], 0.0).then_inc(consts, 1)
            pool.memset(before[:, :], 1.0).then_inc(consts, 1)
            pool.memset(upto[:, :], 1.0).then_inc(consts, 1)
            pool.memset(cmask[:, :], 0.0).then_inc(consts, 1)
            pool.memset(ones[:, :], 1.0).then_inc(consts, 1)
            pool.memset(ones_d[:, :], 1.0 / D).then_inc(consts, 1)
            pool.memset(plus1[:, :], 1.0).then_inc(consts, 1)
            pool.memset(eps[:, :], LN_EPS).then_inc(consts, 1)
            slot1i = hflat[:, 0:SEQ + SLOTS].bitcast(I32)
            pool.iota(slot1i, [[1, SEQ + SLOTS]], base=1 - SLOTS, channel_multiplier=0).then_inc(consts, 1)
            for v in range(PER):
                last = pool.memset(later[:, :, v:v + 1], float(PER - 1 - v))
            last.then_inc(consts, 1)
            pool.wait_ge(consts, 10)
            pool.affine_select(out=ident[:, :], in_=ident[:, :], compare_op=ALU.not_equal, fill=1.0, base=0,
                               pattern=[[1, P]], channel_multiplier=-1).then_inc(consts, 1)
            pool.affine_select(out=before[:, :], in_=before[:, :], compare_op=ALU.is_gt, fill=0.0, base=0,
                               pattern=[[1, P]], channel_multiplier=-1).then_inc(consts, 1)
            pool.affine_select(out=upto[:, :], in_=upto[:, :], compare_op=ALU.is_ge, fill=0.0, base=0,
                               pattern=[[1, P]], channel_multiplier=-1).then_inc(consts, 1)
            pool.affine_select(out=cmask[:, :], in_=cmask[:, :], compare_op=ALU.is_ge, fill=MASKED, base=0,
                               pattern=[[-1, P]], channel_multiplier=1).then_inc(consts, 1)
            pool.tensor_copy(slot1[:, :], slot1i).then_inc(consts, 1)
            pool.wait_ge(consts, CONSTS - 2)
            pool.memset(plus1[0:64, 0:1], 0.0).then_inc(consts, 1)
            pool.wait_ge(consts, CONSTS - 1)
            pool.memset(plus1[64:P, 1:2], 0.0).then_inc(consts, 1)
            steps = 0
            for f in CONV_POOL:
                pool.wait_ge(u_ready, f + 1)
                pool.wait_ge(cols_copied, 1)
                pool.tensor_scalar(CV[:, f, :], U[:, f, 0:SEQ], colv[:, f, 0:1], colv[:, f, ROW_BDW:ROW_BDW + 1],
                                   ALU.mult, ALU.add).then_inc(pchain, 1)
                steps += 1
                for j in range(1, TAPS):
                    pool.tensor_scalar(tap[:, :], U[:, f, j:j + SEQ], colv[:, f, j:j + 1], None,
                                       ALU.mult).then_inc(pchain, 1)
                    pool.wait_ge(pchain, steps + 1)
                    last = pool.tensor_tensor(CV[:, f, :], CV[:, f, :], tap[:, :], ALU.add)
                    if j < TAPS - 1:
                        last.then_inc(pchain, 1)
                        pool.wait_ge(pchain, steps + 2)
                    steps += 2
                last.then_inc(conv_ready, 1)
            pool.wait_ge(spread_used, SPREADS0)
            for r, w in enumerate((ln_mix_g, ln_mix_b, ln_ffn_g, ln_ffn_b)):
                pool.dma_start(lnrows[32 * r:32 * r + 1, :], w[1:2, :]).then_inc(rows_in[1], 16)


        @block.scalar
        def _(act):
            def spread_bias(tile, w, n, signal):
                for q in range(4):
                    src = w.rearrange("(g q n) -> q g n", g=n, q=4)[q:q + 1]
                    act.dma_start(tile[32 * q:32 * q + 32, :, :], src.to_broadcast([32, n, BANK])).then_inc(signal, 16)

            spread_bias(modv[0], b_ada[0], 3, mod0_in)
            for t in range(TT):
                act.dma_start(xs[:, t, :], x[0, t * P:(t + 1) * P, :]).then_inc(x_in, 16)
            act.wait_ge(consts, CONSTS)
            act.wait_ge(cols_copied, 1)
            act.activation(cact[:, :], colv[:, :, ROW_C], ACT.Silu).then_inc(c_acted, 1)
            spread_bias(modv[1], b_ada[1], 3, later_in)
            spread_bias(modkv, b_ada_kv, 1, later_in)
            act.dma_start(brow[0:1, :], b_pw2).then_inc(later_in, 16)
            act.dma_start(rw[:, :, :], router_w.rearrange("(k p) e -> p k e", p=P)).then_inc(later_in, 16)
            act.dma_start(rbias[:, :], router_b.rearrange("(o e) -> o e", o=1).to_broadcast([P, E])).then_inc(later_in, 16)
            act.dma_start(wf[:, :, :], w_kvf[:, 2 * D:2 * D + HEADS].rearrange("(k p) e -> p k e", p=P)).then_inc(later_in, 16)
            act.dma_start(bf[:, :], b_f.rearrange("(h o) -> h o", o=1)).then_inc(later_in, 16)
            for r, w in enumerate((ln_mix_g, ln_mix_b, ln_ffn_g, ln_ffn_b)):
                act.dma_start(lnrows[32 * r:32 * r + 1, :], w[0:1, :]).then_inc(rows_in[0], 16)

            turned = [0]

            def copy_hT():
                for b in (0, 2):
                    act.wait_ge(h_turned, 4 * turned[0] + b + 1)
                    act.activation(hT[:, 2 * b:2 * b + 2, :], PS[:, b, :].rearrange("p (k t) -> p k t", k=2),
                                   ACT.Copy).then_inc(hT_copied, 1)
                turned[0] += 1

            norms = [0]

            def layer_norm_root():
                act.wait_ge(y_ready, norms[0] // TT + 1)
                for t in range(TT):
                    act.activation(hs[:, t, :], PS[:, 2 * t:2 * t + 2, :].rearrange("p b n -> p (b n)"),
                                   ACT.Copy).then_inc(y_read, 1)
                for t in range(TT):
                    act.wait_ge(ln_var, norms[0] + 1)
                    act.activation(rstd[:, t:t + 1], mv[:, t, 1:2], ACT.Sqrt, bias=eps[:, 0:1]).then_inc(ln_sd, 1)
                    norms[0] += 1

            def moe(l):
                act.wait_ge(lmax_ready, l + 1)
                act.activation(r_ex[:, :, :], r_ex[:, :, :], ACT.Exp).then_inc(lexp_ready, 1)

                def take_x(b, n):
                    act.wait_ge(X_summed, n)
                    act.activation(Xg[b], PS[:, X_BANK[b], :], ACT.Copy).then_inc(X_copied, 1)

                def gate(b, n):
                    act.wait_ge(gate_done, n)
                    act.activation(hh[b], PS[:, GATE_BANK[b], :], ACT.Silu).then_inc(sil_ready, 1)

                def take_result(b, n):
                    act.wait_ge(hh_turned, n)
                    act.activation(hhT[b].rearrange("p c s -> p (c s)"), PS[:, HT_BANK[b], :],
                                   ACT.Copy).then_inc(hhT_copied, 1)
                    act.wait_ge(down_done, n)
                    act.activation(yb[b], PS[:, DOWN_BANK[b], :], ACT.Copy).then_inc(yb_copied, 1)

                act.wait_ge(routed, l + 1)
                with act.Fori(0, E) as e:
                    blocks = act.value_load(blocks_i[0:1, bass.ds(e, 1)], min_val=1, max_val=SEQ // SLOTS)
                    with act.If(blocks > 2):
                        with act.Fori(0, blocks - 2):
                            n = act.snap(n_act) + 1
                            take_x(0, n)
                            gate(0, n)
                            take_result(0, n)
                            act.reg_add(n_act, n_act, 1)
                    n = act.snap(n_act) + 1
                    take_x(0, n)
                    with act.If(blocks > 1):
                        take_x(1, n + 1)
                    gate(0, n)
                    with act.If(blocks > 1):
                        gate(1, n + 1)
                    take_result(0, n)
                    with act.If(blocks > 1):
                        take_result(1, n + 1)
                        act.reg_add(n_act, n_act, 1)
                    act.reg_add(n_act, n_act, 1)

            n_act = ctx.enter_context(act.register("blocks_act"))
            act.reg_mov(n_act, 0)
            copy_hT()

            def make_diag(n):
                i, j = divmod(n, TAPS)
                if n >= DIAGS:
                    act.wait_ge(diag_used, n - DIAGS + 1)
                act.activation(diag(n), ident[:, :], ACT.Copy,
                               scale=colv[:, CONV_PE[i], j:j + 1]).then_inc(diag_ready, 1)

            act.wait_ge(h_turned, 4)
            for n in range(DIAGS):
                make_diag(n)
            for f in range(KD):
                act.wait_ge(u_mm, f + 1)
                if f >= 2:
                    act.wait_ge(u_ready, f - 1)
                act.activation(SG[:, f % 2, :], PS[:, f, SEQ:2 * SEQ], ACT.Sigmoid,
                               bias=colv[:, f, ROW_BB:ROW_BB + 1]).then_inc(sig_ready, 1)
            for n in range(DIAGS, len(CONV_PE) * TAPS):
                make_diag(n)
            for i, f in enumerate(CONV_PE):
                act.wait_ge(diag_used, (i + 1) * TAPS)
                act.activation(CV[:, f, :], PS[:, f, 0:SEQ], ACT.Identity,
                               bias=colv[:, f, ROW_BDW:ROW_BDW + 1]).then_inc(conv_ready, 1)
            for k in range(KD):
                act.wait_ge(cen_ready, k + 1)
                act.activation(hflat[:, k * SEQ:(k + 1) * SEQ], CV[:, k, :], ACT.Square).then_inc(sq_ready, 1)
            act.wait_ge(var_done, 1)
            act.activation(crstd, PS[:, 5, 0:SEQ], ACT.Sqrt, bias=eps[:, 0:1]).then_inc(csd_ready, 1)
            for k in range(KD):
                act.wait_ge(cnorm_ready, k + 1)
                act.activation(hT[:, k, :], CV[:, k, :], ACT.Silu, bias=colv[:, k, ROW_LNB:ROW_LNB + 1],
                               scale=colv[:, k, ROW_LNG:ROW_LNG + 1]).then_inc(z_ready, 1)
            layer_norm_root()
            copy_hT()
            moe(0)
            layer_norm_root()
            copy_hT()
            for b in range(4):
                act.wait_ge(k_done, 1)
                act.activation(KT[:, 2 * b:2 * b + 2, :], PS[:, b, :].rearrange("p (k t) -> p k t", k=2),
                               ACT.Copy).then_inc(k_copied, 1)
            act.wait_ge(fz_ready, 1)
            act.activation(fe[0:HEADS, :], fe[0:HEADS, :], ACT.Exp, scale=-1.0).then_inc(fe_ready, 1)
            act.wait_ge(fe_ready, 1)
            act.activation(fe[0:HEADS, :], fe[0:HEADS, :], ACT.Ln, bias=ones[0:HEADS, 0:1]).then_inc(fln_ready, 1)
            copy_hT()
            for b in range(4):
                act.wait_ge(q_done, 1)
                act.activation(QT[:, 2 * b:2 * b + 2, :], PS[:, 4 + b, :].rearrange("p (k t) -> p k t", k=2),
                               ACT.Copy, scale=float(HD) ** -0.5).then_inc(q_copied, 1)

            def probs(h):
                act.wait_ge(nmax_ready, h + 1)
                act.activation(PR[:, h % 3, 0:P], PS[:, 4 + h % 2, 0:P], ACT.Exp, bias=nmax[:, 0, h:h + 1],
                               accum_out=rsum[:, 0, h:h + 1])
                act.activation(PR[:, h % 3, P:3 * P], PS[:, 4 + h % 2, P:3 * P], ACT.Exp,
                               bias=nmax[:, 1, h:h + 1], accum_out=rsum[:, 1, h:h + 1]).then_inc(exp_done, 1)

            def take_o(h):
                act.wait_ge(o_done, h + 1)
                r = HD * (h % 2)
                act.activation(hT[r:r + HD, h // 2, :], PS[r:r + HD, h % 2, 0:SEQ], ACT.Copy).then_inc(o_copied, 1)

            for i in range(HEADS + 3):
                if i < HEADS:
                    probs(i)
                if i >= 3:
                    take_o(i - 3)
            layer_norm_root()
            copy_hT()
            moe(1)
            layer_norm_root()
            for t in range(TT):
                act.wait_ge(x_done, t + 1)
                act.dma_start(out[0, t * P:(t + 1) * P, :], xs[:, t, :]).then_inc(out_done, 16)
            act.wait_ge(out_done, 16 * TT)

        @block.tensor
        def _(pe):
            def quarter(index, k, n):
                return ring[:, index % RING, :].rearrange("p (k f) -> p k f", k=n)[:, k, :]

            def arrived(index, turn=None):
                rounds = index // RING
                if turn is None:
                    pe.wait_ge(landed[index % RING], 16 * (rounds + 1))
                else:
                    pe.wait_ge(landed[index % RING], turn * (16 * TURN // RING) + 16 * (rounds + 1))

            owed = [0]

            def behind(ins):
                if owed[0]:
                    ins.then_inc(half_free, owed[0])
                    owed[0] = 0

            def ada_load(index, j, bank):
                arrived(index + j)
                for kk in range(2):
                    k = 2 * j + kk
                    for q in range(4):
                        last = pe.matmul(PS[32 * q:32 * q + 32, bank, :], crep[:, k, :],
                                         quarter(index + j, kk, 2)[:, q * BANK:(q + 1) * BANK],
                                         start=(k == 0), stop=(k == KD - 1), tile_position=(0, 32 * q))
                        if kk == q == 0:
                            behind(last)
                if j < ADA_G - 1:
                    last.then_inc(half_free, 1)
                else:
                    last.then_inc(ada_done, 1)
                    owed[0] = 1

            def ada(index, bank):
                for j in range(ADA_G):
                    ada_load(index, j, bank)

            spreads = [0]

            def spread_row(row, col=None):
                n = spreads[0]
                if n >= 2:
                    pe.wait_ge(spread_used, n - 1)
                for i in range(2):
                    r, v = row(i)
                    last = pe.matmul(PS[:, 4 + 2 * (n % 2) + i, :], ones[r:r + 1, :], v, start=True, stop=True)
                    if i == 0:
                        behind(last)
                last.then_inc(spread, 1)
                spreads[0] += 1

            def spread_mod(tile, v):
                def row(i):
                    q = 2 * (v % 2) + i
                    return 32 * q, tile[32 * q:32 * q + 1, v // 2, :]
                spread_row(row)

            def spread_ln(r):
                spread_row(lambda i: (32 * r, lnrows[32 * r:32 * r + 1, i * BANK:(i + 1) * BANK]))

            hs_turned = [0]

            def turn_h():
                n = hs_turned[0]
                pe.wait_ge(h_ready, 2 * n + 2)
                for b in range(4):
                    for k in (2 * b, 2 * b + 1):
                        for t in range(TT):
                            last = pe.transpose(PS[:, b, (k % 2) * SEQ + t * P:(k % 2) * SEQ + (t + 1) * P],
                                                hs[:, t, k * P:(k + 1) * P], ident[:, :])
                    last.then_inc(h_turned, 1)
                hs_turned[0] += 1
                pe.wait_ge(hT_copied, 4 * (n + 1))

            def project(index, banks, done=None, chunk_ready=None):
                for h in range(2):
                    arrived(index + h)
                    for kk in range(KH):
                        k = KH * h + kk
                        if chunk_ready is not None:
                            pe.wait_ge(chunk_ready, k + 1)
                        for t in range(TT):
                            for q in range(2):
                                last = pe.matmul(PS[:, banks + 2 * t + q, :], hT[:, k, t * P:(t + 1) * P],
                                                 quarter(index + h, kk, KH)[:, q * BANK:(q + 1) * BANK],
                                                 start=(k == 0), stop=(k == KD - 1 and done is not None))
                                if k == t == q == 0:
                                    behind(last)
                    if h == 0 or done is None:
                        last.then_inc(half_free, 1)
                if done is not None:
                    last.then_inc(done, 1)
                    owed[0] = 1

            def project_T(index, banks, done):
                for h in range(2):
                    arrived(index + h)
                    for kk in range(KH):
                        k = KH * h + kk
                        for f in range(KD):
                            last = pe.matmul(PS[:, banks + f // 2, (f % 2) * SEQ:(f % 2 + 1) * SEQ],
                                             quarter(index + h, kk, KH)[:, f * P:(f + 1) * P], hT[:, k, :],
                                             start=(k == 0 and f % 2 == 0), stop=(k == KD - 1),
                                             skip_group_check=True)
                            if k == f == 0:
                                behind(last)
                    if h == 0:
                        last.then_inc(half_free, 1)
                last.then_inc(done, 1)
                owed[0] = 1

            def norm_spreads(l, which, ada_index=None):
                spread_mod(modv[l], (2, 5)[which])
                if ada_index is not None:
                    pe.wait_ge(y_read, TT * (2 * l + which + 1))
                    ada(ada_index, 0)
                pe.wait_ge(rows_in[l], ROWS)
                spread_ln(2 * which)
                spread_ln(2 * which + 1)

            def moe(index, l):
                for t in range(TT):
                    for k in range(KD):
                        last = pe.matmul(PS[:, B_GATE, t * E:(t + 1) * E], hT[:, k, t * P:(t + 1) * P],
                                         rw[:, k, :], start=(k == 0), stop=(k == KD - 1))
                last.then_inc(logits_done, 1)
                def zero_sums():
                    for b in range(4):
                        behind(pe.matmul(PS[:, b, :], ident[0:1, 1:2].to_broadcast([1, P]), hs[0:1, 0, 0:BANK],
                                         start=True, stop=False, skip_group_check=True))

                if l > 0:
                    zero_sums()
                if l == 0:
                    for j in range(ADA_G // 2):
                        ada_load(L_ADA1_G0, j, B_Y)
                pe.wait_ge(sel_ready, l + 1)
                pe.matmul(PS[:, B_UP, 0:E], before[:, :], r_sel[:, 0, :], start=True, stop=True)
                pe.matmul(PS[:, B_UP, E:2 * E], ones[:, :], r_sel[:, 0, :], start=True, stop=False)
                pe.matmul(PS[:, B_UP, E:2 * E], before[:, :], r_sel[:, 1, :], start=False, stop=True)
                pe.matmul(PS[0:1, B_M, 0:E], ones[:, 0:1], r_sel[:, 0, :], start=True, stop=False)
                pe.matmul(PS[0:1, B_M, 0:E], ones[:, 0:1], r_sel[:, 1, :], start=False,
                          stop=True).then_inc(pos_done, 1)
                if l == 0:
                    for j in range(ADA_G // 2, ADA_G):
                        ada_load(L_ADA1_G0, j, B_Y)
                if l == 0:
                    zero_sums()
                    pe.wait_ge(ada_added, 5)

                def sum_x(b, n, frees):
                    pe.wait_ge(G_built, n)
                    for t in range(TT):
                        for q in range(2):
                            last = pe.matmul(PS[SLOTS * q:SLOTS * (q + 1), X_BANK[b], :], G[b][:, t, :],
                                             hs[:, t, q * BANK:(q + 1) * BANK], start=(t == 0),
                                             stop=(t == TT - 1), tile_position=(0, SLOTS * q),
                                             skip_group_check=True)
                            if frees and t == q == 0:
                                last.then_inc(half_free, frees)
                    last.then_inc(X_summed, 1)

                def turn_x(b, n):
                    pe.wait_ge(X_copied, n)
                    for cc in range(KH):
                        last = pe.transpose(PS[:, XT_BANK[b], cc * P:(cc + 1) * P], Xg[b][:, cc * P:(cc + 1) * P],
                                            ident[:, :])
                    last.then_inc(X_turned, 1)
                    pe.wait_ge(XT_copied, n)

                def product(load, turn, bank, stationary, done, frees):
                    for h in range(2):
                        arrived(load + h, turn)
                        for kk in range(KH):
                            for q in range(2):
                                last = pe.matmul(PS[SLOTS * q:SLOTS * (q + 1), bank, :],
                                                 stationary[:, kk, SLOTS * h:SLOTS * (h + 1)],
                                                 quarter(load + h, kk, KH)[:, q * BANK:(q + 1) * BANK],
                                                 start=(h == 0 and kk == 0), stop=(h == 1 and kk == KH - 1),
                                                 tile_position=(0, SLOTS * q), skip_group_check=True)
                                if frees and h == kk == q == 0:
                                    last.then_inc(half_free, frees)
                    last.then_inc(done, 1)

                def down(b, n, load, turn, frees):
                    pe.wait_ge(hh_ready, n)
                    for cc in range(KH):
                        last = pe.transpose(PS[:, HT_BANK[b], cc * P:(cc + 1) * P], hh[b][:, cc * P:(cc + 1) * P],
                                            ident[:, :])
                        if frees and cc == 0:
                            last.then_inc(half_free, frees)
                    last.then_inc(hh_turned, 1)
                    for t in range(TT):
                        last = pe.transpose(PS[:, GWT_BANK[b], t * P:(t + 1) * P],
                                            GW[b][:, t, :, :].rearrange("p q s -> p (q s)"), ident[:, :])
                    last.then_inc(GW_turned, 1)
                    pe.wait_ge(hhT_copied, n)
                    pe.wait_ge(GWT_copied, n)
                    product(load, turn, DOWN_BANK[b], hhT[b], down_done, 0)

                def combine(b, n, frees):
                    pe.wait_ge(yb_copied, n)
                    for t in range(TT):
                        for q in range(2):
                            last = pe.matmul(PS[:, 2 * t + q, :],
                                             GWT[b][SLOTS * q:SLOTS * (q + 1), t * P:(t + 1) * P],
                                             yb[b][SLOTS * q:SLOTS * (q + 1), :], start=False, stop=False,
                                             skip_group_check=True)
                            if frees and t == q == 0:
                                last.then_inc(half_free, frees)

                def expert(index, turn, blocks, closes_turn):
                    gate_w, up_w, down_w = index, index + 2, index + 4
                    with pe.If(blocks > 2):
                        with pe.Fori(0, blocks - 2):
                            n = pe.snap(n_pe) + 1
                            turn_x(0, n)
                            product(gate_w, turn, GATE_BANK[0], XT[0], gate_done, 0)
                            product(up_w, turn, UP_BANK[0], XT[0], up_done, 0)
                            down(0, n, down_w, turn, 0)
                            sum_x(0, n + 1, 0)
                            combine(0, n, 0)
                            pe.reg_add(n_pe, n_pe, 1)
                    n = pe.snap(n_pe) + 1
                    turn_x(0, n)
                    with pe.If(blocks > 1):
                        sum_x(1, n + 1, 0)
                        turn_x(1, n + 1)
                    product(gate_w, turn, GATE_BANK[0], XT[0], gate_done, 0)
                    with pe.If(blocks > 1):
                        product(gate_w, turn, GATE_BANK[1], XT[1], gate_done, 0)
                    product(up_w, turn, UP_BANK[0], XT[0], up_done, 2)
                    with pe.If(blocks > 1):
                        product(up_w, turn, UP_BANK[1], XT[1], up_done, 0)
                    down(0, n, down_w, turn, 2)
                    with pe.If(blocks > 1):
                        down(1, n + 1, down_w, turn, 0)
                        combine(1, n + 1, 0)
                        pe.reg_add(n_pe, n_pe, 1)
                    pe.reg_add(n_pe, n_pe, 1)
                    following = pe.snap(n_pe) + 1
                    if closes_turn:
                        with pe.If(turn < E // UNROLL - 1):
                            sum_x(0, following, 0)
                        combine(0, n, 2)
                    else:
                        sum_x(0, following, 2)
                        combine(0, n, 0)

                pe.wait_ge(routed, l + 1)
                sum_x(0, pe.snap(n_pe) + 1, 0)
                with pe.Fori(0, E // UNROLL) as turn:
                    for i in range(UNROLL):
                        blocks = pe.value_load(blocks_i[0:1, bass.ds(turn * UNROLL + i, 1)], min_val=1,
                                               max_val=SEQ // SLOTS)
                        expert(index + 6 * i, turn, blocks, i == UNROLL - 1)
                for b in range(4):
                    last = pe.matmul(PS[:, b, 0:1], ident[0:1, 1:2].to_broadcast([1, P]), hs[0:1, 0, 0:1],
                                     start=False, stop=True, skip_group_check=True)
                last.then_inc(y_ready, 1)

            n_pe = ctx.enter_context(pe.register("blocks_pe"))
            pe.reg_mov(n_pe, 0)
            pe.wait_ge(consts, CONSTS)
            pe.wait_ge(colrows_in, COLROWS)
            for k in range(KD):
                last = pe.transpose(PS[:, B_Y, k * 40:k * 40 + NROWS], colrows[0:NROWS, k * P:(k + 1) * P],
                                    ident[0:NROWS, 0:NROWS])
            last.then_inc(cols_turned, 1)
            pe.wait_ge(c_spread, 1)
            ada(L_ADA0_G0, 0)
            pe.wait_ge(ada_added, 1)
            spread_mod(modv[0], 1)
            spread_mod(modv[0], 0)
            turn_h()
            for f in range(KD):
                for g in range(2):
                    for j in range(4):
                        if f == g == 0:
                            arrived(L_PW1 + j)
                        for kk in range(2):
                            k = 2 * j + kk
                            last = pe.matmul(PS[:, f, g * SEQ:(g + 1) * SEQ],
                                             quarter(L_PW1 + j, kk, 2)[:, g * D + f * P:g * D + (f + 1) * P],
                                             hT[:, k, :], start=(k == 0), stop=(k == KD - 1), skip_group_check=True)
                            if f == KD - 1 and g == 1 and kk == 1 and j < 3:
                                last.then_inc(half_free, 1)
                last.then_inc(u_mm, 1)
            owed[0] = 1
            pe.wait_ge(u_ready, 1)
            ada(L_ADA0_G1, 0)
            for i, f in enumerate(CONV_PE):
                pe.wait_ge(u_ready, f + 1)
                for j in range(TAPS):
                    n = i * TAPS + j
                    pe.wait_ge(diag_ready, n + 1)
                    last = pe.matmul(PS[:, f, 0:SEQ], diag(n), U[:, f, j:j + SEQ], start=(j == 0), stop=(j == TAPS - 1))
                    last.then_inc(diag_used, 1)
            ada(L_ADA0_G2, 1)
            for k in range(KD):
                if k == 0:
                    pe.wait_ge(conv_ready, KD)
                last = pe.matmul(PS[:, 4, 0:SEQ], ones_d[:, :], CV[:, k, :], start=(k == 0), stop=(k == KD - 1))
                if k == 0:
                    behind(last)
            last.then_inc(mean_done, 1)
            for k in range(KD):
                pe.wait_ge(sq_ready, k + 1)
                last = pe.matmul(PS[:, 5, 0:SEQ], ones_d[:, :], hflat[:, k * SEQ:(k + 1) * SEQ],
                                 start=(k == 0), stop=(k == KD - 1))
            last.then_inc(var_done, 1)
            pe.wait_ge(ada_added, 3)
            pe.wait_ge(later_in, LATER)
            project(L_PW2, 0, chunk_ready=z_ready)
            for t in range(TT):
                for q in range(2):
                    last = pe.matmul(PS[:, 2 * t + q, :], ones[0:1, :], brow[0:1, q * BANK:(q + 1) * BANK],
                                     start=False, stop=True)
            last.then_inc(y_ready, 1)
            norm_spreads(0, 0, L_ADAKV)
            pe.wait_ge(ada_added, 4)
            spread_mod(modv[0], 4)
            spread_mod(modv[0], 3)
            turn_h()
            moe(L_MOE0, 0)
            norm_spreads(0, 1, L_ADA1_G1)
            spread_mod(modkv, 1)
            spread_mod(modkv, 0)
            pe.wait_ge(ada_added, 6)
            turn_h()
            spread_mod(modv[1], 1)
            spread_mod(modv[1], 0)
            project_T(L_WK, 0, k_done)
            pe.wait_ge(spread_used, SPREADS0 + 4)
            project(L_WV, 4, v_done)
            pe.wait_ge(k_copied, 4)
            for k in range(KD):
                last = pe.matmul(PS[0:HEADS, 0, 0:SEQ], wf[:, k, :], hT[:, k, :], start=(k == 0), stop=(k == KD - 1))
                if k == 0:
                    behind(last)
            last.then_inc(f_done, 1)
            pe.wait_ge(fz_ready, 1)
            turn_h()
            pe.wait_ge(v_copied, 4)
            pe.wait_ge(logf_ready, 1)
            project_T(L_WQ, 4, q_done)
            for t in range(TT):
                last = pe.transpose(PS[:, 0, t * HEADS:(t + 1) * HEADS], fl[0:HEADS, t * P:(t + 1) * P],
                                    ident[0:HEADS, 0:HEADS])
                if t == 0:
                    behind(last)
            last.then_inc(logf_turned, 1)
            pe.wait_ge(ltok_copied, 1)
            pe.matmul(PS[:, 1, 0:HEADS], upto[:, :], ltok[:, 0, :], start=True, stop=True)
            pe.matmul(PS[:, 1, HEADS:2 * HEADS], ones[:, :], ltok[:, 0, :], start=True, stop=False)
            pe.matmul(PS[:, 1, HEADS:2 * HEADS], upto[:, :], ltok[:, 1, :], start=False, stop=True)
            pe.matmul(PS[0:HEADS, 2, 0:P], ltok[:, 0, :], upto[:, :], start=True, stop=True)
            pe.matmul(PS[0:HEADS, 2, P:2 * P], ltok[:, 0, :], ones[:, :], start=True, stop=False)
            pe.matmul(PS[0:HEADS, 2, P:2 * P], ltok[:, 1, :], upto[:, :], start=False, stop=True).then_inc(fcum_done, 1)
            pe.wait_ge(fcum_copied, 1)
            pe.wait_ge(q_copied, 4)

            def scores(h):
                if h >= 2:
                    pe.wait_ge(exp_done, h - 1)
                b, r, hp = 4 + h % 2, HD * (h % 2), h // 2
                one_h = ident[0:HEADS, h:h + 1].to_broadcast([HEADS, P])
                for t in range(TT):
                    o, n = (0, P, 3 * P)[t], (t + 1) * P
                    pe.matmul(PS[:, b, o:o + n], QT[r:r + HD, hp, t * P:(t + 1) * P], KT[r:r + HD, hp, 0:n],
                              start=True, stop=False, skip_group_check=True)
                    pe.matmul(PS[:, b, o:o + n], one_h, nfc[0:HEADS, 0:n], start=False, stop=False,
                              skip_group_check=True)
                    last = pe.matmul(PS[:, b, o + n - P:o + n], ident[:, :], cmask[:, :], start=False, stop=True,
                                     skip_group_check=True)
                last.then_inc(s_done, 1)

            def turn_probs(h):
                pe.wait_ge(p_ready, h + 1)
                for i in range(3):
                    last = pe.transpose(PS[:, 2 + h % 2, i * P:(i + 1) * P], PR[:, h % 3, i * P:(i + 1) * P], ident[:, :])
                last.then_inc(p_turned, 1)

            def weigh(h):
                pe.wait_ge(pT_copied, h + 1)
                if h >= 2:
                    pe.wait_ge(o_copied, h - 1)
                r = HD * (h % 2)
                o = PS[r:r + HD, h % 2, :]
                v = V[:, :, h * HD:(h + 1) * HD]
                pe.matmul(o[:, 0:P], v[:, 0, :], PRT[:, h % 2, 0:P], start=True, stop=True)
                pe.matmul(o[:, P:2 * P], v[:, 0, :], PRT[:, h % 2, P:2 * P], start=True, stop=False)
                pe.matmul(o[:, P:2 * P], v[:, 1, :], PRT[:, h % 2, 2 * P:3 * P], start=False,
                          stop=True).then_inc(o_done, 1)

            for i in range(HEADS + 3):
                if i < HEADS:
                    scores(i)
                if 2 <= i < HEADS + 2:
                    turn_probs(i - 2)
                if i >= 3:
                    weigh(i - 3)
                if i < ADA_G:
                    ada_load(L_ADA1_G2, i, 6)
            pe.wait_ge(o_copied, HEADS)
            project(L_WO, 0, y_ready)
            pe.wait_ge(ada_added, 7)
            norm_spreads(1, 0)
            spread_mod(modv[1], 4)
            spread_mod(modv[1], 3)
            turn_h()
            moe(L_MOE1, 1)
            norm_spreads(1, 1)

        @block.vector
        def _(dve):
            chain = [0]

            def link(ins):
                chain[0] += 1
                ins.then_inc(dchain, 1)
                dve.wait_ge(dchain, chain[0])

            turned, adas, spreads, norms, ys = [0], [0], [0], [0], [0]

            def copy_hT():
                for b in (1, 3):
                    dve.wait_ge(h_turned, 4 * turned[0] + b + 1)
                    dve.tensor_copy(hT[:, 2 * b:2 * b + 2, :],
                                    PS[:, b, :].rearrange("p (k t) -> p k t", k=2)).then_inc(hT_copied, 1)
                turned[0] += 1

            def add_ada(tile, g, bank):
                adas[0] += 1
                dve.wait_ge(ada_done, adas[0])
                dve.scalar_tensor_tensor(out=tile[:, g, :], in0=tile[:, g, :], scalar=plus1[:, g:g + 1],
                                         in1=PS[:, bank, :], op0=ALU.add, op1=ALU.add).then_inc(ada_added, 1)

            def spread_banks():
                n = spreads[0]
                dve.wait_ge(spread, n + 1)
                spreads[0] += 1
                b = 4 + 2 * (n % 2)
                return PS[:, b:b + 2, :].rearrange("p b n -> p (b n)")

            def with_row(dst, src, op, done=None):
                row = spread_banks()
                for t in range(TT):
                    last = dve.tensor_tensor(dst[:, t, :], src[:, t, :], row, op)
                    if done is not None:
                        last.then_inc(done, 1)
                if done is not None:
                    return
                last.then_inc(spread_used, 1)
                dve.wait_ge(spread_used, spreads[0])

            def modulate():
                with_row(hs, xs, ALU.mult)
                row = spread_banks()
                for t in range(TT):
                    dve.tensor_tensor(hs[:, t, :], hs[:, t, :], row, ALU.add).then_inc(h_ready, 1)
                hn[0] += 2
                dve.wait_ge(h_ready, hn[0])
                dve.sem_inc(spread_used, 1)

            hn = [0]

            def close_sublayer(ada_next=None, done=None):
                ys[0] += 1
                row = spread_banks()
                for t in range(TT):
                    dve.wait_ge(y_read, 2 * (ys[0] - 1) + t + 1)
                    last = dve.tensor_tensor(hs[:, t, :], hs[:, t, :], row, ALU.mult)
                last.then_inc(spread_used, 1)
                dve.wait_ge(spread_used, spreads[0])
                for t in range(TT):
                    last = dve.scalar_tensor_tensor(out=xs[:, t, :], in0=xs[:, t, :], scalar=ALPHA, in1=hs[:, t, :],
                                                    op0=ALU.mult, op1=ALU.add)
                link(last)
                for t in range(TT):
                    for q in range(2):
                        last = dve.bn_stats(stats[:, t, q, :], xs[:, t, q * BANK:(q + 1) * BANK])
                link(last)
                for t in range(TT):
                    dve.bn_aggr(mv[:, t, :], stats[:, t, :, :].rearrange("p q s -> p (q s)")).then_inc(ln_var, 1)
                norms[0] += 2
                dve.wait_ge(ln_sd, norms[0])
                link(dve.reciprocal(rstd[:, :], rstd[:, :]))
                for t in range(TT):
                    last = dve.tensor_scalar(xs[:, t, :], xs[:, t, :], mv[:, t, 0:1], rstd[:, t:t + 1],
                                             ALU.subtract, ALU.mult)
                link(last)
                if ada_next is not None:
                    add_ada(*ada_next, 0)
                with_row(xs, xs, ALU.mult)
                with_row(xs, xs, ALU.add, done)

            def ranks(rank, compared, values, n):
                for d in range(1, n):
                    link(dve.tensor_tensor(compared[:, :, 0:n - d], values[:, :, 0:n - d], values[:, :, d:n], ALU.is_ge))
                    link(dve.tensor_tensor(rank[:, :, d:n], rank[:, :, d:n], compared[:, :, 0:n - d], ALU.add))
                    link(dve.tensor_tensor(rank[:, :, 0:n - d], rank[:, :, 0:n - d], compared[:, :, 0:n - d], ALU.subtract))

            def moe(l):
                lg = PS[:, B_GATE, 0:TT * E].rearrange("p (t e) -> p t e", t=TT)
                dve.wait_ge(logits_done, l + 1)
                link(dve.tensor_tensor(r_p[:, :, :], lg, rbias[:, :].unsqueeze(1).to_broadcast([P, TT, E]), ALU.add))
                link(dve.tensor_reduce(r_s[:, :], r_p[:, :, :], AX.X, ALU.max))
                dve.tensor_tensor(r_ex[:, :, :], r_p[:, :, :], r_s[:, :].unsqueeze(2).to_broadcast([P, TT, E]),
                                  ALU.subtract).then_inc(lmax_ready, 1)
                dve.wait_ge(lexp_ready, l + 1)
                link(dve.tensor_reduce(r_s[:, :], r_ex[:, :, :], AX.X, ALU.add))
                link(dve.reciprocal(r_s[:, :], r_s[:, :]))
                link(dve.tensor_tensor(r_p[:, :, :], r_ex[:, :, :], r_s[:, :].unsqueeze(2).to_broadcast([P, TT, E]), ALU.mult))
                pg = r_p[:, :, :].rearrange("p t (g i) -> p (t g) i", g=GROUPS)
                selg = r_sel[:, :, :].rearrange("p t (g i) -> p (t g) i", g=GROUPS)
                wg = r_w[:, :, :].rearrange("p t (g i) -> p (t g) i", g=GROUPS)
                link(dve.tensor_copy(r_rk[:, :, :], later[:, :, :]))
                ranks(r_rk, r_c, pg, PER)
                link(dve.tensor_scalar(selg, r_rk[:, :, :], 2.0, None, ALU.is_lt))
                link(dve.tensor_tensor(wg, pg, selg, ALU.mult))
                link(dve.tensor_reduce(r_gs[:, :, :].rearrange("p t g -> p (t g)"), wg, AX.X, ALU.add))
                link(dve.tensor_copy(r_gr[:, :, :], later[:, 0:TT, :]))
                ranks(r_gr, r_gc, r_gs, GROUPS)
                link(dve.tensor_scalar(r_gs[:, :, :], r_gr[:, :, :], 1.0, None, ALU.is_lt))
                gb = r_gs[:, :, :].rearrange("p t g -> p (t g)").unsqueeze(2).to_broadcast([P, 2 * GROUPS, PER])
                dve.tensor_tensor(selg, selg, gb, ALU.mult).then_inc(sel_ready, 1)
                link(dve.tensor_tensor(wg, wg, gb, ALU.mult))
                link(dve.tensor_reduce(r_s[:, :], r_w[:, :, :], AX.X, ALU.add))
                link(dve.reciprocal(r_s[:, :], r_s[:, :]))
                link(dve.tensor_tensor(r_w[:, :, :], r_w[:, :, :], r_s[:, :].unsqueeze(2).to_broadcast([P, TT, E]), ALU.mult))
                dve.wait_ge(pos_done, l + 1)
                dve.wait_ge(sel_ready, l + 1)
                link(dve.scalar_tensor_tensor(out=r_pos[:, :, :],
                                              in0=PS[:, B_UP, 0:TT * E].rearrange("p (t e) -> p t e", t=TT),
                                              scalar=1.0, in1=r_sel[:, :, :], op0=ALU.add, op1=ALU.mult))
                cnt = PS[0:1, B_M, 0:E]
                link(dve.tensor_scalar(r_n[:, :], cnt, float(SLOTS), 1.0, ALU.is_gt, ALU.add))
                for m in range(2, SEQ // SLOTS):
                    dst = r_n if m < SEQ // SLOTS - 1 else blocks_i
                    link(dve.scalar_tensor_tensor(out=dst[:, :], in0=cnt, scalar=float(m * SLOTS), in1=r_n[:, :],
                                                  op0=ALU.is_gt, op1=ALU.add))
                dve.sem_inc(routed, 1)
                if l == 0:
                    add_ada(modv[1], 0, B_Y)

                def build(b, e, end_slot):
                    slots = slot1[:, bass.ds(end_slot, SLOTS)]
                    for t in range(TT):
                        dve.tensor_scalar(G[b][:, t, :], slots, r_pos[:, t, bass.ds(e, 1)], None, ALU.is_equal)
                    for t in range(TT):
                        for q in range(2):
                            last = dve.tensor_scalar(GW[b][:, t, q, :], slots, r_pos[:, t, bass.ds(e, 1)],
                                                     r_w[:, t, bass.ds(e, 1)], ALU.is_equal, ALU.mult)
                    last.then_inc(G_built, 1)

                def take_xT(b, n):
                    dve.wait_ge(X_turned, n)
                    dve.tensor_copy(XT[b].rearrange("p c s -> p (c s)"), PS[:, XT_BANK[b], :]).then_inc(XT_copied, 1)

                def times_up(b, n):
                    dve.wait_ge(sil_ready, n)
                    dve.wait_ge(up_done, n)
                    dve.tensor_tensor(hh[b], hh[b], PS[:, UP_BANK[b], :], ALU.mult).then_inc(hh_ready, 1)

                def take_weights(b, n):
                    dve.wait_ge(GW_turned, n)
                    dve.tensor_copy(GWT[b], PS[:, GWT_BANK[b], 0:SEQ]).then_inc(GWT_copied, 1)

                dve.wait_ge(routed, l + 1)
                with dve.Fori(0, E) as e:
                    blocks = dve.value_load(blocks_i[0:1, bass.ds(e, 1)], min_val=1, max_val=SEQ // SLOTS)
                    with dve.If(blocks > 2):
                        with dve.Fori(0, blocks - 2) as j:
                            n = dve.snap(n_dve) + 1
                            build(0, e, (j + 1) * SLOTS)
                            take_xT(0, n)
                            times_up(0, n)
                            take_weights(0, n)
                            dve.reg_add(n_dve, n_dve, 1)
                    n = dve.snap(n_dve) + 1
                    build(0, e, blocks * SLOTS)
                    take_xT(0, n)
                    with dve.If(blocks > 1):
                        build(1, e, (blocks - 1) * SLOTS)
                        take_xT(1, n + 1)
                    times_up(0, n)
                    with dve.If(blocks > 1):
                        times_up(1, n + 1)
                    take_weights(0, n)
                    with dve.If(blocks > 1):
                        take_weights(1, n + 1)
                        dve.reg_add(n_dve, n_dve, 1)
                    dve.reg_add(n_dve, n_dve, 1)

            n_dve = ctx.enter_context(dve.register("blocks_dve"))
            dve.reg_mov(n_dve, 0)
            link(dve.memset(U[:, :, 0:PAD], 0.0))
            dve.wait_ge(consts, CONSTS)
            dve.wait_ge(cols_turned, 1)
            dve.tensor_copy(colv[:, :, :], PS[:, B_Y, 0:KD * 40].rearrange("p (k r) -> p k r", r=40)[:, :, 0:NROWS]).then_inc(cols_copied, 1)
            dve.wait_ge(c_acted, 1)
            dve.tensor_copy(crep[:, :, :], cact[:, :].unsqueeze(2).to_broadcast([P, KD, 32])).then_inc(c_spread, 1)
            dve.wait_ge(mod0_in, 16 * 4)
            add_ada(modv[0], 0, 0)
            dve.wait_ge(x_in, 16 * TT)
            modulate()
            copy_hT()
            dve.wait_ge(cols_copied, 1)
            tap_done = {}
            for step, f, *taps in DVE_STEPS:
                if step == "u":
                    dve.wait_ge(sig_ready, f + 1)
                    dve.scalar_tensor_tensor(out=U[:, f, PAD:PAD + SEQ], in0=PS[:, f, 0:SEQ],
                                             scalar=colv[:, f, ROW_BA:ROW_BA + 1], in1=SG[:, f % 2, :],
                                             op0=ALU.add, op1=ALU.mult).then_inc(u_ready, 1)
                    continue
                for j in range(*taps):
                    for fc in f:
                        if j == 0:
                            dve.wait_ge(u_ready, fc + 1)
                            ins = dve.tensor_scalar(CV[:, fc, :], U[:, fc, 0:SEQ], colv[:, fc, 0:1],
                                                    colv[:, fc, ROW_BDW:ROW_BDW + 1], ALU.mult, ALU.add)
                        else:
                            dve.wait_ge(dchain, tap_done[fc])
                            ins = dve.scalar_tensor_tensor(out=CV[:, fc, :], in0=U[:, fc, j:j + SEQ],
                                                           scalar=colv[:, fc, j:j + 1], in1=CV[:, fc, :],
                                                           op0=ALU.mult, op1=ALU.add)
                        if j < TAPS - 1:
                            chain[0] += 1
                            tap_done[fc] = chain[0]
                            ins.then_inc(dchain, 1)
                        else:
                            ins.then_inc(conv_ready, 1)
            add_ada(modv[0], 1, 0)
            add_ada(modv[0], 2, 1)
            dve.wait_ge(later_in, LATER)
            dve.wait_ge(conv_ready, KD)
            dve.wait_ge(mean_done, 1)
            for k in range(KD):
                dve.tensor_tensor(CV[:, k, :], CV[:, k, :], PS[:, 4, 0:SEQ], ALU.subtract).then_inc(cen_ready, 1)
            dve.wait_ge(cen_ready, KD)
            dve.wait_ge(csd_ready, 1)
            link(dve.reciprocal(crstd, crstd))
            for k in range(KD):
                dve.tensor_tensor(CV[:, k, :], CV[:, k, :], crstd, ALU.mult).then_inc(cnorm_ready, 1)
            close_sublayer((modkv, 0))
            modulate()
            copy_hT()
            moe(0)
            close_sublayer((modv[1], 1))
            modulate()
            copy_hT()
            modulate()
            for t in range(TT):
                for q in range(2):
                    dve.wait_ge(v_done, 1)
                    dve.tensor_copy(V[:, t, q * BANK:(q + 1) * BANK], PS[:, 4 + 2 * t + q, :]).then_inc(v_copied, 1)
            dve.wait_ge(f_done, 1)
            link(dve.tensor_scalar(fz[0:HEADS, :], PS[0:HEADS, 0, 0:SEQ], bf[:, 0:1], None, ALU.add))
            link(dve.tensor_scalar(fe[0:HEADS, :], fz[0:HEADS, :], -1.0, None, ALU.mult))
            dve.tensor_tensor(fe[0:HEADS, :], fe[0:HEADS, :], fz[0:HEADS, :], ALU.max).then_inc(fz_ready, 1)
            dve.wait_ge(fln_ready, 1)
            dve.scalar_tensor_tensor(out=fl[0:HEADS, :], in0=fz[0:HEADS, :], scalar=0.0, in1=fe[0:HEADS, :],
                                     op0=ALU.min, op1=ALU.subtract).then_inc(logf_ready, 1)
            copy_hT()
            dve.wait_ge(logf_turned, 1)
            dve.tensor_copy(ltok, PS[:, 0, 0:TT * HEADS].rearrange("p (t h) -> p t h", t=TT)).then_inc(ltok_copied, 1)
            dve.wait_ge(fcum_done, 1)
            dve.tensor_scalar(nfc[0:HEADS, :], PS[0:HEADS, 2, 0:SEQ], -1.0, None, ALU.mult)
            link(dve.tensor_copy(fq, PS[:, 1, 0:TT * HEADS].rearrange("p (t h) -> p t h", t=TT)))
            dve.sem_inc(fcum_copied, 1)

            def row_max(h):
                b = 4 + h % 2
                dve.wait_ge(s_done, h + 1)
                dve.tensor_reduce(rmax[:, 0, h:h + 1], PS[:, b, 0:P], AX.X, ALU.max)
                link(dve.tensor_reduce(rmax[:, 1, h:h + 1], PS[:, b, P:3 * P], AX.X, ALU.max))
                link(dve.tensor_tensor(rmax[:, :, h], rmax[:, :, h], fq[:, :, h], ALU.add))
                dve.tensor_tensor(nmax[:, :, h], fq[:, :, h], rmax[:, :, h], ALU.subtract).then_inc(nmax_ready, 1)

            def normalise(h):
                dve.wait_ge(exp_done, h + 1)
                link(dve.reciprocal(rinv[:, :, h], rsum[:, :, h]))
                dve.tensor_scalar(PR[:, h % 3, 0:P], PR[:, h % 3, 0:P], rinv[:, 0, h:h + 1], None, ALU.mult)
                dve.tensor_scalar(PR[:, h % 3, P:3 * P], PR[:, h % 3, P:3 * P], rinv[:, 1, h:h + 1], None,
                                  ALU.mult).then_inc(p_ready, 1)

            def copy_pT(h):
                dve.wait_ge(p_turned, h + 1)
                dve.tensor_copy(PRT[:, h % 2, :], PS[:, 2 + h % 2, 0:3 * P]).then_inc(pT_copied, 1)

            for i in range(HEADS + 3):
                if i >= 3:
                    copy_pT(i - 3)
                if 1 <= i <= HEADS:
                    normalise(i - 1)
                if i < HEADS:
                    row_max(i)
            add_ada(modv[1], 2, 6)
            close_sublayer()
            modulate()
            copy_hT()
            moe(1)
            close_sublayer(done=x_done)


_INS = ["x", "c", "w_ada", "b_ada", "ln_mix_g", "ln_mix_b", "ln_ffn_g", "ln_ffn_b",
        "w_pw1", "b_pw1", "w_dw", "b_dw", "conv_ln_g", "conv_ln_b", "w_pw2", "b_pw2",
        "w_ada_kv", "b_ada_kv", "w_kvf", "b_f", "w_q", "w_o",
        "router_w", "router_b", "w_gate", "w_up", "w_down"]


def kernel(**inputs):
    import numpy as _np
    import concourse.bacc as _bacc
    from concourse import mybir as _mybir
    from concourse.bass_utils import run_bass_kernel_spmd as _run

    nc = _bacc.Bacc("TRN2", target_bir_lowering=False, num_devices=1)
    arrays, args = {}, []
    for name in _INS:
        a = _np.ascontiguousarray(inputs[name])
        arrays[f"in_{name}_dram"] = a
        args.append(nc.dram_tensor(f"in_{name}_dram", a.shape, _mybir.dt.from_np(a.dtype), kind="ExternalInput").ap())
    shape = arrays["in_x_dram"].shape
    args.append(nc.dram_tensor("out_0_dram", shape, _mybir.dt.float32, kind="ExternalOutput").ap())
    trunk_kernel(nc, *args)
    r = _run(nc, [arrays], core_ids=[0])
    return r.results[0]["out_0_dram"]
```
